# Optimizing a Trainium2 kernel written in Bass

```python
import jax, jax.numpy as jnp
from jax import lax
import numpy as np

D_MODEL = 1024
BATCH = 1
SEQ = 1024
DEPTH = 1
DEC_BATCH = 8
DEC_SEQ = 4
PAST_LEN = 1024
PAGE_SIZE = 128

D_MIX = D_MODEL
MLA_HEADS = 8
QK_NOPE_DIM = 64
QK_ROPE_DIM = 32
QK_HEAD_DIM = QK_NOPE_DIM + QK_ROPE_DIM
V_HEAD_DIM = 64
Q_LORA_RANK = 256
KV_LORA_RANK = 128
MLA_WIDTH = MLA_HEADS * V_HEAD_DIM
RET_HEADS = 8
RET_DK = 64
RET_DV = 64
RET_WIDTH = RET_HEADS * RET_DV
RET_CHUNK = 128
ROPE_THETA = 10000.0
QUERY_BLOCK = 128
IN_SIZES = (Q_LORA_RANK, KV_LORA_RANK, QK_ROPE_DIM, RET_HEADS * RET_DK, RET_HEADS * RET_DK, RET_HEADS * RET_DV, RET_WIDTH)
D_IN = sum(IN_SIZES)
PEER_KEYS = 128
PEER_EXPERTS = PEER_KEYS * PEER_KEYS
PEER_HEADS = 8
PEER_QDIM = 256
PEER_TOPK = 16
PEER_BLOCK = 256
EPS = 1e-6

kernel_name = "hymba_mla_retnet_peer_step"

def rms_norm(x, w):
    xf = x.astype(jnp.float32)
    y = xf * lax.rsqrt(jnp.mean(xf * xf, -1, keepdims=True) + EPS)
    return (y * w.astype(jnp.float32)).astype(x.dtype)

def rope(x, pos):
    half = x.shape[-1] // 2
    inv = ROPE_THETA ** (-jnp.arange(half, dtype=jnp.float32) / half)
    ang = pos.astype(jnp.float32)[:, None] * inv[None, :]
    cos = jnp.cos(ang)[:, None, :]
    sin = jnp.sin(ang)[:, None, :]
    x1, x2 = x[..., :half], x[..., half:]
    return jnp.concatenate([x1 * cos - x2 * sin, x1 * sin + x2 * cos], -1).astype(x.dtype)

def mixer_inputs(x, pos, attn_norm_w, w_in, q_a_norm_w, w_uq, q_norm_w, kv_a_norm_w):
    xn = rms_norm(x, attn_norm_w)
    offsets = [int(o) for o in np.cumsum(IN_SIZES)[:-1]]
    q_lat, c_kv, k_pe, rq, rk, rv, rg = jnp.split(xn @ w_in, offsets, axis=-1)
    lead = x.shape[:-1]
    q = (rms_norm(q_lat, q_a_norm_w) @ w_uq).reshape(lead + (MLA_HEADS, QK_HEAD_DIM))
    q = rms_norm(q, q_norm_w)
    q = jnp.concatenate([q[..., :QK_NOPE_DIM], rope(q[..., QK_NOPE_DIM:], pos)], -1)
    c_kv = rms_norm(c_kv, kv_a_norm_w)
    rq = rope(rq.reshape(lead + (RET_HEADS, RET_DK)), pos)
    rk = rope(rk.reshape(lead + (RET_HEADS, RET_DK)), pos) * (RET_DK ** -0.5)
    rv = rv.reshape(lead + (RET_HEADS, RET_DV))
    return q, c_kv, k_pe, rq, rk, rv, rg

def mla_kv(c_kv, k_pe, w_ukv, k_norm_w, pos):
    kv = (c_kv @ w_ukv).reshape(c_kv.shape[:-1] + (MLA_HEADS, QK_NOPE_DIM + V_HEAD_DIM))
    k_nope, v = kv[..., :QK_NOPE_DIM], kv[..., QK_NOPE_DIM:]
    k_pe_h = jnp.broadcast_to(k_pe[..., None, :], k_nope.shape[:-1] + (QK_ROPE_DIM,)).astype(k_nope.dtype)
    k = rms_norm(jnp.concatenate([k_nope, k_pe_h], -1), k_norm_w)
    k = jnp.concatenate([k[..., :QK_NOPE_DIM], rope(k[..., QK_NOPE_DIM:], pos)], -1)
    return k, v

def attend(q, k, v, q_pos, k_pos):
    s = jnp.einsum('...qhd,...khd->...hqk', q, k, preferred_element_type=jnp.float32) * (QK_HEAD_DIM ** -0.5)
    s = jnp.where(k_pos[None, :] <= q_pos[:, None], s, -jnp.inf)
    p = jax.nn.softmax(s, axis=-1).astype(v.dtype)
    return jnp.einsum('...hqk,...khd->...qhd', p, v)

def prompt_mla(q, c_kv, k_pe, pos, w_ukv, k_norm_w):
    b, t = q.shape[:2]
    k, v = mla_kv(c_kv, k_pe, w_ukv, k_norm_w, pos)
    nb = t // QUERY_BLOCK
    q_blocks = q.reshape(b, nb, QUERY_BLOCK, MLA_HEADS, QK_HEAD_DIM).swapaxes(0, 1)
    pos_blocks = pos.reshape(nb, QUERY_BLOCK)
    out = lax.map(lambda a: attend(a[0], k, v, a[1], pos), (q_blocks, pos_blocks))
    return out.swapaxes(0, 1).reshape(b, t, MLA_WIDTH)

def sample_mla(q, c_all, pe_all, q_pos, k_pos, w_ukv, k_norm_w):
    def one(a):
        q_s, c_s, p_s = a
        k, v = mla_kv(c_s, p_s, w_ukv, k_norm_w, k_pos)
        return attend(q_s, k, v, q_pos, k_pos)
    out = lax.map(one, (q, c_all, pe_all))
    return out.reshape(q.shape[0], q.shape[1], MLA_WIDTH)

def ret_log_decay():
    return jnp.log1p(-jnp.power(2.0, -5.0 - jnp.arange(RET_HEADS, dtype=jnp.float32)))

def retention_chunk(R, qkv):
    q, k, v = qkv
    q = q.astype(jnp.float32); k = k.astype(jnp.float32); v = v.astype(jnp.float32)
    c = q.shape[1]
    lg = ret_log_decay()
    i = jnp.arange(c, dtype=jnp.float32)
    diff = i[:, None] - i[None, :]
    dmat = jnp.where(diff >= 0, jnp.exp(lg[:, None, None] * jnp.maximum(diff, 0.0)), 0.0)
    inner = jnp.einsum('bihd,bjhd->bhij', q, k) * dmat
    o = jnp.einsum('bhij,bjhv->bihv', inner, v)
    cross = jnp.exp(lg[None, :] * (i[:, None] + 1.0))
    o = o + jnp.einsum('bihd,bhdv->bihv', q, R) * cross[None, :, :, None]
    k_dec = jnp.exp(lg[None, :] * (c - 1.0 - i[:, None]))
    R_new = jnp.exp(lg * c)[None, :, None, None] * R + jnp.einsum('bjhd,bjhv->bhdv', k * k_dec[None, :, :, None], v)
    return R_new, o

def retention(q, k, v, R0, chunk):
    b, t = q.shape[:2]
    nc = t // chunk
    def to_chunks(a):
        return a.reshape((b, nc, chunk) + a.shape[2:]).swapaxes(0, 1)
    R, o = lax.scan(retention_chunk, R0, (to_chunks(q), to_chunks(k), to_chunks(v)))
    return o.swapaxes(0, 1).reshape(b, t, RET_HEADS, RET_DV), R

def head_group_norm(o, w):
    mu = jnp.mean(o, -1, keepdims=True)
    var = jnp.mean(jnp.square(o - mu), -1, keepdims=True)
    y = (o - mu) * lax.rsqrt(var + EPS)
    return y.reshape(o.shape[:-2] + (RET_WIDTH,)) * w.astype(jnp.float32)

def peer_block(xb, w_peer_q, sub_keys1, sub_keys2, peer_u, peer_v):
    n = xb.shape[0]
    q = (xb @ w_peer_q).reshape(n, PEER_HEADS, 2, PEER_QDIM // 2)
    s1 = jnp.einsum('nhd,kd->nhk', q[:, :, 0], sub_keys1, preferred_element_type=jnp.float32)
    s2 = jnp.einsum('nhd,kd->nhk', q[:, :, 1], sub_keys2, preferred_element_type=jnp.float32)
    v1, i1 = lax.top_k(s1, PEER_TOPK)
    v2, i2 = lax.top_k(s2, PEER_TOPK)
    cand = (v1[..., :, None] + v2[..., None, :]).reshape(n, PEER_HEADS, PEER_TOPK * PEER_TOPK)
    vs, ic = lax.top_k(cand, PEER_TOPK)
    e1 = jnp.take_along_axis(i1, ic // PEER_TOPK, axis=-1)
    e2 = jnp.take_along_axis(i2, ic % PEER_TOPK, axis=-1)
    experts = e1 * PEER_KEYS + e2
    g = jax.nn.softmax(vs, axis=-1).astype(xb.dtype)
    act = jax.nn.gelu(jnp.einsum('nd,nhkd->nhk', xb, peer_u[experts]), approximate=False)
    return jnp.einsum('nhk,nhkd->nd', g * act, peer_v[experts])

def peer(x, w_peer_q, sub_keys1, sub_keys2, peer_u, peer_v):
    shape = x.shape
    xf = x.reshape(-1, D_MODEL)
    n = xf.shape[0]
    nb = -(-n // PEER_BLOCK)
    xp = jnp.pad(xf, ((0, nb * PEER_BLOCK - n), (0, 0))).reshape(nb, PEER_BLOCK, D_MODEL)
    out = lax.map(lambda b: peer_block(b, w_peer_q, sub_keys1, sub_keys2, peer_u, peer_v), xp)
    return out.reshape(nb * PEER_BLOCK, D_MODEL)[:n].reshape(shape)

def output_and_ffn(x, mla_out, ret_o, rg, ret_norm_w, w_o, ffn_norm_w, w_peer_q, sub_keys1, sub_keys2, peer_u, peer_v):
    ret_out = jax.nn.silu(rg) * head_group_norm(ret_o, ret_norm_w).astype(x.dtype)
    h = x + jnp.concatenate([mla_out.astype(x.dtype), ret_out], -1) @ w_o
    return h + peer(rms_norm(h, ffn_norm_w), w_peer_q, sub_keys1, sub_keys2, peer_u, peer_v)

def setup_inputs(seed: int = 0) -> dict:
    key = jax.random.key(seed)
    ks = jax.random.split(key, 24)
    n_pages = PAST_LEN // PAGE_SIZE
    n_used = DEC_BATCH * n_pages
    n_pool = n_used + n_used // 4
    def nrm(k, shape, scale):
        return jax.random.normal(k, shape, jnp.float32) * scale
    def gain(k, shape):
        return 1.0 + 0.02 * jax.random.normal(k, shape, jnp.float32)
    page_table = jax.random.permutation(ks[0], n_pool)[:n_used].reshape(DEC_BATCH, n_pages).astype(jnp.int32)
    return {
        'x_prompt': nrm(ks[1], (BATCH, SEQ, D_MODEL), 1.0),
        'x_sample': nrm(ks[2], (DEC_BATCH, DEC_SEQ, D_MODEL), 1.0),
        'cache_kv_latent': nrm(ks[3], (DEPTH, n_pool, PAGE_SIZE, KV_LORA_RANK), 1.0),
        'cache_k_rope': nrm(ks[4], (DEPTH, n_pool, PAGE_SIZE, QK_ROPE_DIM), 1.0),
        'state_ret': nrm(ks[5], (DEPTH, DEC_BATCH, RET_HEADS, RET_DK, RET_DV), 0.5),
        'page_table': page_table,
        'attn_norm_w': gain(ks[6], (DEPTH, D_MODEL)),
        'w_in': nrm(ks[7], (DEPTH, D_MODEL, D_IN), D_MODEL ** -0.5),
        'q_a_norm_w': gain(ks[8], (DEPTH, Q_LORA_RANK)),
        'w_uq': nrm(ks[9], (DEPTH, Q_LORA_RANK, MLA_HEADS * QK_HEAD_DIM), Q_LORA_RANK ** -0.5),
        'q_norm_w': gain(ks[10], (DEPTH, QK_HEAD_DIM)),
        'kv_a_norm_w': gain(ks[11], (DEPTH, KV_LORA_RANK)),
        'w_ukv': nrm(ks[12], (DEPTH, KV_LORA_RANK, MLA_HEADS * (QK_NOPE_DIM + V_HEAD_DIM)), KV_LORA_RANK ** -0.5),
        'k_norm_w': gain(ks[13], (DEPTH, QK_HEAD_DIM)),
        'ret_norm_w': gain(ks[14], (DEPTH, RET_WIDTH)),
        'w_o': nrm(ks[15], (DEPTH, D_MIX, D_MODEL), D_MIX ** -0.5),
        'ffn_norm_w': gain(ks[16], (DEPTH, D_MODEL)),
        'w_peer_q': nrm(ks[17], (DEPTH, D_MODEL, PEER_HEADS * PEER_QDIM), D_MODEL ** -0.5),
        'peer_sub_keys1': nrm(ks[18], (DEPTH, PEER_KEYS, PEER_QDIM // 2), (PEER_QDIM // 2) ** -0.5),
        'peer_sub_keys2': nrm(ks[19], (DEPTH, PEER_KEYS, PEER_QDIM // 2), (PEER_QDIM // 2) ** -0.5),
        'peer_u': nrm(ks[20], (DEPTH, PEER_EXPERTS, D_MODEL), D_MODEL ** -0.5),
        'peer_v': nrm(ks[21], (DEPTH, PEER_EXPERTS, D_MODEL), 0.3),
    }

def reference(x_prompt, x_sample, cache_kv_latent, cache_k_rope, state_ret, page_table,
              attn_norm_w, w_in, q_a_norm_w, w_uq, q_norm_w, kv_a_norm_w, w_ukv, k_norm_w,
              ret_norm_w, w_o, ffn_norm_w, w_peer_q, peer_sub_keys1, peer_sub_keys2, peer_u, peer_v):
    n_seq_s = x_sample.shape[0]
    pos_p = jnp.arange(SEQ)
    pos_s = PAST_LEN + jnp.arange(DEC_SEQ)
    pos_all = jnp.arange(PAST_LEN + DEC_SEQ)
    hp, hs = x_prompt, x_sample
    lat_p, pe_p, R_p, lat_s, pe_s, R_s = [], [], [], [], [], []
    for l in range(DEPTH):
        mix_w = (attn_norm_w[l], w_in[l], q_a_norm_w[l], w_uq[l], q_norm_w[l], kv_a_norm_w[l])
        out_w = (ret_norm_w[l], w_o[l], ffn_norm_w[l], w_peer_q[l], peer_sub_keys1[l], peer_sub_keys2[l], peer_u[l], peer_v[l])
        q, c_kv, k_pe, rq, rk, rv, rg = mixer_inputs(hp, pos_p, *mix_w)
        mla_out = prompt_mla(q, c_kv, k_pe, pos_p, w_ukv[l], k_norm_w[l])
        R0 = jnp.zeros((hp.shape[0], RET_HEADS, RET_DK, RET_DV), jnp.float32)
        ret_o, R_new = retention(rq, rk, rv, R0, RET_CHUNK)
        hp = output_and_ffn(hp, mla_out, ret_o, rg, *out_w)
        lat_p.append(c_kv); pe_p.append(k_pe); R_p.append(R_new)
        q, c_kv, k_pe, rq, rk, rv, rg = mixer_inputs(hs, pos_s, *mix_w)
        past_lat = cache_kv_latent[l][page_table].reshape(n_seq_s, PAST_LEN, KV_LORA_RANK)
        past_pe = cache_k_rope[l][page_table].reshape(n_seq_s, PAST_LEN, QK_ROPE_DIM)
        c_all = jnp.concatenate([past_lat.astype(c_kv.dtype), c_kv], axis=1)
        pe_all = jnp.concatenate([past_pe.astype(k_pe.dtype), k_pe], axis=1)
        mla_out = sample_mla(q, c_all, pe_all, pos_s, pos_all, w_ukv[l], k_norm_w[l])
        ret_o, R_new = retention(rq, rk, rv, state_ret[l].astype(jnp.float32), DEC_SEQ)
        hs = output_and_ffn(hs, mla_out, ret_o, rg, *out_w)
        lat_s.append(c_kv); pe_s.append(k_pe); R_s.append(R_new)
    return (hp, hs, jnp.stack(lat_p), jnp.stack(pe_p), jnp.stack(R_p), jnp.stack(lat_s), jnp.stack(pe_s), jnp.stack(R_s))


_drawn_inputs = setup_inputs


def setup_inputs(seed=0):
    import zlib

    import numpy as np

    out = dict(_drawn_inputs(seed))
    spreads = {}
    factors = {'q_a_norm_w': 8.0,
     'q_norm_w': 7.205,
     'k_norm_w': 8.0,
     'ret_norm_w': 3.692,
     'ffn_norm_w': 2.708}
    for name, (base, spread) in spreads.items():
        noise = np.random.default_rng([zlib.crc32(name.encode()), seed]).standard_normal(out[name].shape)
        drawn = base * np.exp(spread * noise) if base else spread * noise
        out[name] = __import__('jax').numpy.asarray(drawn.astype(out[name].dtype))
    for name, factor in factors.items():
        out[name] = (out[name] * factor).astype(out[name].dtype)
    return out
```

```python
from contextlib import ExitStack

import concourse.bass as bass
from concourse import mybir

ALU = mybir.AluOpType
ACT = mybir.ActivationFunctionType
F32 = mybir.dt.float32
I32 = mybir.dt.int32
U32 = mybir.dt.uint32
AX_X = mybir.AxisListType.X

P = 128
D = 1024
DC = D // P
TILES = 8
ST = 32
SEQS, STEPS = 8, 4
PAGES = 8
H = 8
NOPE, ROPE = 64, 32
QK = NOPE + ROPE
QR, KVR = 256, 128
LAT = QR + KVR + ROPE
K = 16
SLOTS = H * K
DIAGS = 4
RING = 8
PIECE = 256
N_IN, N_LAT, N_O, N_PQ = 10, 2, 4, 8
O_0 = N_IN + N_LAT
PQ_0 = O_0 + N_O
PIECES = PQ_0 + N_PQ
EPS = 1e-6
SCALE = QK ** -0.5
LOWEST = -3.0e38


class Steps:

    def __init__(self, eng, sem):
        self.eng, self.sem, self.n, self.last = eng, sem, 0, None

    def done(self, instruction):
        instruction.then_inc(self.sem, 1)
        self.n += 1
        self.last = (self.sem, self.n)

    def raises(self, instruction, sem, value):
        instruction.then_inc(sem, 1)
        self.last = (sem, value)

    def wait(self, behind=0):
        if self.last is None:
            return
        sem, value = self.last
        if behind:
            assert sem is self.sem
            if value > behind:
                self.eng.wait_ge(sem, value - behind)
        else:
            self.eng.wait_ge(sem, value)

    def close(self):
        self.wait()
        self.eng.sem_inc(self.sem, 1)
        self.eng.wait_ge(self.sem, self.n + 1)
        self.eng.sem_clear(self.sem)
        self.n, self.last = 0, None


def over(ap, axis, shape):
    return ap.unsqueeze(axis).to_broadcast(shape)


def hybrid_decoder_step(nc, x_prompt, x_sample, cache_latent, cache_rope, state, page_table,
                        attn_w, weights, qa_w, q_w, kva_w, w_ukT, k_w, ret_w,
                        ffn_w, keys1T, keys2T, experts,
                        rope_rows, rope_pages, mask_rows, mask_new, decay_in, decay_cross, decay_k,
                        decay_state, s_decay_in, s_decay_cross, s_decay_k, s_decay_state, s_same,
                        eye,
                        y_prompt, y_sample, lat_prompt, pe_prompt, R_prompt, lat_sample, pe_sample,
                        R_sample):
    with ExitStack() as ctx:
        def sb(name, shape, dt=F32):
            return ctx.enter_context(nc.sbuf_tensor(name, shape, dt))

        def sem(name):
            return ctx.enter_context(nc.semaphore(name))

        ps = ctx.enter_context(nc.psum_tensor("ps", [P, 8, 512], F32))
        acc = ps[:, 0:2, :]

        def bank(i, n=P, w=512):
            return ps[0:n, 2 + i, 0:w]

        ident = sb("ident", [P, P])
        attn_wc = sb("attn_wc", [P, DC])
        qa_wc = sb("qa_wc", [P, 2])
        q_wb = sb("q_wb", [P, QK])
        k_wb = sb("k_wb", [P, QK])
        kva_wb = sb("kva_wb", [P, KVR])
        ret_wb = sb("ret_wb", [P, 512])
        k1T = sb("k1T", [P, P])
        k2T = sb("k2T", [P, P])
        dec_cross = sb("dec_cross", [P, H])
        dec_k = sb("dec_k", [P, H])
        dec_state = sb("dec_state", [P, 4])
        iota16 = sb("iota16", [P, K])
        passing = sb("passing", [P, 1])
        ptab = sb("ptab", [1, SEQS * PAGES], I32)

        resid = sb("resid", [P, D])
        rope_t = sb("rope_t", [P, 192])
        table = sb("table", [P, D])
        wbuf = sb("wbuf", [P, 2, DC, PIECE])
        xT = sb("xT", [P, DC, P])
        mix = sb("mix", [P, D])
        ss = sb("ss", [P, 4])
        lat = sb("lat", [P, LAT])
        latn = sb("latn", [P, QR + KVR])
        latT = sb("latT", [P, 3, P])
        kT = sb("kT", [P, H, D])
        vN = sb("vN", [P, TILES, 512])
        qT = sb("qT", [P, H, P])
        rq = sb("rq", [P, 512])
        rk = sb("rk", [P, 512])
        rv = sb("rv", [P, 512])
        rg = sb("rg", [P, 512])
        th = sb("th", [P, 512])
        R = sb("R", [P, 4, 64])
        root_x = sb("root_x", [P, 72])
        root_y = sb("root_y", [P, 72])
        root_t = sb("root_t", [P, 72])
        ms8 = sb("ms8", [P, 16])
        mx = sb("mx", [P, H])
        nb = sb("nb", [P, H])
        sums = sb("sums", [P, H])
        xn_next = sb("xn_next", [P, D])
        vals = sb("vals", [P, 2, K])
        idx8 = sb("idx8", [P, 2, K], U32)
        top_c = sb("top_c", [P, K], U32)
        ab = sb("ab", [P, 2, K], U32)
        e12 = sb("e12", [P, 2, K])
        top_v = sb("top_v", [P, H, K])
        gate_x = sb("gate_x", [P, H, K])
        codes_next = sb("codes_next", [P, SLOTS], U32)
        gates_next = sb("gates_next", [P, SLOTS])
        arena = sb("arena", [P, 4352])
        junk = arena[:, 3072:4096]
        junk_lat = arena[:, 4096:4352]
        qbuf = arena[:, 0:768].rearrange("p (h d) -> p h d", h=H)
        sqq = arena[:, 768:1536]
        kbuf = arena[:, 1536:2304].rearrange("p (h d) -> p h d", h=H)
        sqk = arena[:, 2304:2816]
        kpw = arena[:, 2816:2848]
        kpr = arena[:, 2848:2880]
        ropet = arena[:, 2880:3392]
        kd = arena[:, 3392:3904]
        inT = arena[:, 0:1024].rearrange("p (h i) -> p h i", h=H)
        crossv = arena[:, 1024:1536]
        oret = arena[:, 1536:2048]
        rqT = arena[:, 1536:2048].rearrange("p (r q) -> p r q", r=4)
        rkT = arena[:, 2048:2560].rearrange("p (r q) -> p r q", r=4)
        osq = arena[:, 2048:2560]
        scores = arena[:, 0:2048].rearrange("p (b k) -> p b k", b=2)
        probT = arena[:, 2048:4096].rearrange("p (b k) -> p b k", b=2)
        pq = arena[:, 0:512].rearrange("p (b k) -> p b k", b=2)
        sS = arena[:, 512:1024].rearrange("p (b j k) -> p b j k", b=2, j=2)
        sS2 = arena[:, 1024:1280].rearrange("p (j k) -> p j k", j=2)
        cand = arena[:, 1280:1536]
        cand2 = arena[:, 1536:1792]
        hot = arena[:, 1792:2304].rearrange("p (a k j) -> p a k j", a=2, k=K)
        ybuf = arena[:, 0:1024]

        ring = sb("ring", [P, RING, 2 * D])
        h_cur = sb("h_cur", [P, D])
        xn_cur = sb("xn_cur", [P, D])
        codes = sb("codes", [P, SLOTS], U32)
        gates = sb("gates", [P, SLOTS])
        dots = sb("dots", [P, SLOTS])
        gelus = sb("gelus", [P, SLOTS])
        coefs = sb("coefs", [P, SLOTS])
        diag = sb("diag", [P, DIAGS, P])

        dec_in = table[:, :].rearrange("p (h i) -> p h i", h=H)
        uq = wbuf[:, N_IN % 2].rearrange("p c n -> p (c n)")[:, 0:2 * 768].rearrange("p (c n) -> p c n", c=2)
        ukv = wbuf[:, (N_IN + 1) % 2].rearrange("p c n -> p (c n)")
        uk, uv = ukv[:, 0:512], ukv[:, 512:1024]

        kflat = kT[:, :, :].rearrange("p h k -> p (h k)")
        pg = kflat[:, 0:2560].rearrange("p (b j c) -> p b j c", b=2, j=PAGES)
        cT = kflat[:, 2560:3584]
        kpT = kflat[:, 3584:4608]
        sqn = kflat[:, 4608:5632].rearrange("p (b c) -> p b c", b=2)
        kp2 = kflat[:, 5632:6144].rearrange("p (j c) -> p j c", j=PAGES)
        kpt = kflat[:, 6144:6400].rearrange("p (j c) -> p j c", j=PAGES)
        sT = kflat[:, 6400:6688]
        pT = kflat[:, 6688:6976]
        prob = kflat[:, 6976:8004]
        vflat = vN[:, :, :].rearrange("p t c -> p (t c)")
        Rs = vflat[:, 0:2048].rearrange("p (r b v) -> p r b v", r=4, b=SEQS)
        QT = vflat[:, 2048:2304].rearrange("p (b h s) -> p b h s", b=SEQS, h=H)
        QPT = vflat[:, 2304:2560].rearrange("p (b h s) -> p b h s", b=SEQS, h=H)
        OL = vflat[:, 2560:2816].rearrange("p (h b s) -> p h b s", h=H, b=SEQS)
        qnT = vflat[:, 2816:2944].rearrange("p (r t) -> p r t", r=4)
        kp2n = vflat[:, 2944:3008]
        kpTn = vflat[:, 3008:3040]
        ss_k = vflat[:, 3040:3112]
        rpages = vflat[:, 3112:3624].rearrange("p (j c) -> p j c", j=PAGES)
        ol = vflat[:, 3624:3752]
        qp = vflat[:, 3752:4008]
        s4 = vflat[:, 4008:4012]
        mask4 = vflat[:, 4012:4016]
        ones32 = vflat[:, 4016:4024]
        smx = vflat[:, 4024:4032]
        dec_in_s = table[:, 640:896]
        wkT = table[:, 0:512].rearrange("p (r l) -> p r l", r=4)
        cross_s = table[:, 512:576].rearrange("p (h b) -> p h b", h=H)
        same_s = table[:, 576:584]
        dec_state_s = table[:, 584:588]
        dec_k_s = table[:, 588:596]
        cnew = xT[0:STEPS]

        const_in = sem("const_in")
        const_set = sem("const_set")
        tile_in = sem("tile_in")
        w_in_buf = [sem("w_even_in"), sem("w_odd_in")]
        piece_done = sem("piece_done")
        vec = sem("vector_steps")
        act_s = sem("scalar_steps")
        squares = sem("squares")
        wide_ready = sem("wide_ready")
        turned = sem("turned")
        xT_a = sem("xT_a")
        xT_b = sem("xT_b")
        lat_ready = sem("lat_ready")
        lat_stored = sem("lat_stored")
        latT_ps = sem("latT_ps")
        latT_ready = sem("latT_ready")
        rg_ready = sem("rg_ready")
        mask_in = sem("mask_in")
        ffn_in = sem("ffn_in")
        v_ready = sem("v_ready")
        qk_ready = sem("qk_ready")
        qT_ps = sem("qT_ps")
        kT_ps = sem("kT_ps")
        qT_ready = sem("qT_ready")
        kT_ready = sem("kT_ready")
        rT_ps = sem("rT_ps")
        rT_ready = sem("rT_ready")
        inner_ps = sem("inner_ps")
        inner_ready = sem("inner_ready")
        cross_ps = sem("cross_ps")
        R_ready = sem("R_ready")
        o_ps = sem("o_ps")
        o_taken = sem("o_taken")
        scores_ps = sem("scores_ps")
        scores_ready = sem("scores_ready")
        prob_ready = sem("prob_ready")
        probT_ps = sem("probT_ps")
        probT_a = sem("probT_a")
        probT_b = sem("probT_b")
        pv_ps = sem("pv_ps")
        h_ready = sem("h_ready")
        pq_ready = sem("pq_ready")
        keys_ps = sem("keys_ps")
        keys_copied = sem("keys_copied")
        keys_used = sem("keys_used")
        gate_in = sem("gate_in")
        gate_exp = sem("gate_exp")
        handed = sem("handed")
        h_moved = sem("h_moved")
        row_in = [sem(f"row_in_{i}") for i in range(RING)]
        dot_done = sem("dot_done")
        gelu_done = sem("gelu_done")
        coef_done = sem("coef_done")
        diag_ready = sem("diag_ready")
        row_free = sem("row_free")
        y_ready = sem("y_ready")
        y_stored = sem("y_stored")
        R_stored = sem("R_stored")
        s_const_in = sem("s_const_in")
        s_set = sem("s_set")
        s_state_in = sem("s_state_in")
        s_cnew_in = sem("s_cnew_in")
        s_q_ready = sem("s_q_ready")
        s_q_ps = sem("s_q_ps")
        s_q_copied = sem("s_q_copied")
        s_ql_ps = sem("s_ql_ps")
        s_ql_ready = sem("s_ql_ready")
        s_cross_ps = sem("s_cross_ps")
        s_cross_taken = sem("s_cross_taken")
        s_vexp = sem("s_vexp")
        s_R_ps = sem("s_R_ps")
        s_R_ready = sem("s_R_ready")
        s_R_stored = sem("s_R_stored")
        pages_in = [sem("pages_even_in"), sem("pages_odd_in")]
        kp2_ready = sem("kp2_ready")
        pageT_ps = sem("pageT_ps")
        cT_ready = sem("cT_ready")
        kpT_ready = sem("kpT_ready")
        kn_ps = sem("kn_ps")
        kn_sq = sem("kn_sq")
        kn_taken = sem("kn_taken")
        sT_ps = sem("sT_ps")
        sT_ready = sem("sT_ready")
        s_ps = sem("s_ps")
        s_max = sem("s_max")
        s_prob = sem("s_prob")
        s_pT_ps = sem("s_pT_ps")
        s_pT = sem("s_pT")
        s_o_ps = sem("s_o_ps")
        s_o = sem("s_o")
        s_oT_ps = sem("s_oT_ps")
        s_oT = sem("s_oT")

        N_CONST = 13

        def prompt_slots():
            sizes = [8, 2] + [2] * N_IN + [2, 2] + [2, 2, 2, 2] + [2, 2, 2, 2] + [4] * (H + 2)
            sizes += [4, 4, 2] + [2, 2] + [0, 0, 0] + [2, 2, 0, 2, 0, 0] * (H // 2)
            sizes.append(SLOTS - sum(sizes))
            return sizes

        def sample_slots():
            sizes = [8, 2] + [2] * N_IN + [2, 2] + [2, 2] + [6] * SEQS + [2, 2, 2] + [2, 2] + [0, 0, 0] + [2, 2, 0] * H
            sizes.append(SLOTS - sum(sizes))
            return sizes

        passed = {nc.vector: sem("vector_passed"), nc.gpsimd: sem("pool_passed"), nc.sync: sem("sync_passed")}

        def apart(eng):
            eng.sem_inc(passed[eng], 1)

        block = ctx.enter_context(nc.Block())

        @block.sync
        def _(sp):
            for dst, src in ((ident, eye), (attn_wc, attn_w), (qa_wc, qa_w),
                             (q_wb, q_w.partition_broadcast(P)), (k_wb, k_w.partition_broadcast(P)),
                             (kva_wb, kva_w.partition_broadcast(P)),
                             (ret_wb, ret_w.partition_broadcast(P)), (k1T, keys1T), (k2T, keys2T),
                             (dec_cross, decay_cross), (dec_k, decay_k),
                             (dec_state, decay_state), (ptab, page_table)):
                sp.dma_start(dst[:], src).then_inc(const_in, 16)

            def load_tile(t):
                if isinstance(t, int) and t == 0:
                    pass
                else:
                    sp.wait_ge(h_moved, t)
                sp.dma_start(resid[:], x_prompt[bass.ds(t * P, P), :]).then_inc(tile_in, 16)
                sp.dma_start(rope_t[:], rope_rows[bass.ds(t * P, P), :]).then_inc(tile_in, 16)
                sp.dma_start(table[:], decay_in).then_inc(tile_in, 16)

            def load_piece(t, w):
                if not (isinstance(t, int) and t == 0 and w < 2):
                    sp.wait_ge(piece_done, t * PIECES + w - 1)
                sp.dma_start(wbuf[:, w % 2].rearrange("p c n -> p (c n)"), weights[w]).then_inc(w_in_buf[w % 2], 16)

            def store_latents(t, latent, pe, n):
                sp.wait_ge(lat_ready, t + 1)
                sp.dma_start(latent, latn[0:n, QR:QR + KVR]).then_inc(lat_stored, 16)
                sp.dma_start(pe, lat[0:n, QR + KVR:LAT]).then_inc(lat_stored, 16)

            def store_y(t, y, n):
                sp.wait_ge(y_ready, t + 1)
                sp.dma_start(y, ybuf[0:n]).then_inc(y_stored, 16)

            def load_mask(t):
                sp.wait_ge(inner_ready, t + 1)
                apart(sp)
                sp.dma_start(table[:], mask_rows[:, bass.ds((TILES - 1 - t) * P, D)]).then_inc(mask_in, 16)

            def front(t):
                load_tile(t)
                for w in range(O_0):
                    load_piece(t, w)
                store_latents(t, lat_prompt[bass.ds(t * P, P), :], pe_prompt[bass.ds(t * P, P), :], P)
                load_mask(t)
                for w in range(O_0, O_0 + 2):
                    load_piece(t, w)
                sp.wait_ge(scores_ready, H * (t + 1))
                apart(sp)
                sp.dma_start(table[:], ffn_w.partition_broadcast(P)).then_inc(ffn_in, 16)
                for w in range(O_0 + 2, PIECES):
                    load_piece(t, w)

            front(0)
            with sp.Fori(0, TILES - 1) as i:
                front(i + 1)
                store_y(i, y_prompt[bass.ds(i * P, P), :], P)
            sp.wait_ge(h_moved, TILES)
            sp.dma_start(resid[0:ST], x_sample).then_inc(tile_in, 16)
            sp.dma_start(rope_t[0:ST], rope_rows[TILES * P:TILES * P + ST, :]).then_inc(tile_in, 16)
            sp.dma_start(wkT, w_ukT).then_inc(tile_in, 16)
            for dst, src in ((cross_s[0:ST], s_decay_cross), (same_s[0:ST], s_same),
                             (dec_state_s, s_decay_state), (dec_k_s[0:ST], s_decay_k),
                             (dec_in_s[0:ST], s_decay_in), (rpages, rope_pages), (mask4[0:ST], mask_new)):
                sp.dma_start(dst, src).then_inc(s_const_in, 16)
            for r in range(4):
                for b in range(SEQS):
                    sp.dma_start(Rs[:, r, b, :], state[b, 2 * r:2 * r + 2].rearrange("h k v -> (h k) v")).then_inc(s_state_in, 16)

            def load_pages(b):
                if b >= 2:
                    sp.wait_ge(s_o, b - 1)
                for j in range(PAGES):
                    page = sp.value_load(ptab[0:1, b * PAGES + j:b * PAGES + j + 1], min_val=0,
                                         max_val=cache_latent.shape[0] - 1)
                    sp.dma_start(pg[:, b % 2, j, 0:KVR], cache_latent[bass.ds(page, 1)].rearrange("o p c -> (o p) c")).then_inc(pages_in[b % 2], 16)
                    sp.dma_start(pg[:, b % 2, j, KVR:], cache_rope[bass.ds(page, 1)].rearrange("o p c -> (o p) c")).then_inc(pages_in[b % 2], 16)

            load_pages(0)
            load_pages(1)
            for w in range(O_0):
                load_piece(TILES, w)
            store_latents(TILES, lat_sample, pe_sample, ST)
            for b in range(SEQS):
                sp.dma_start(cnew[:, b, :], latn[b * STEPS:(b + 1) * STEPS, QR:QR + KVR]).then_inc(s_cnew_in, 16)
            for b in range(2, SEQS):
                load_pages(b)
            sp.wait_ge(s_R_ready, 4)
            for b in range(SEQS):
                for r in range(4):
                    sp.dma_start(R_sample[b, 2 * r:2 * r + 2].rearrange("h k v -> (h k) v"), Rs[:, r, b, :]).then_inc(s_R_stored, 16)
            sp.dma_start(R_prompt.rearrange("(r h) k v -> (h k) r v", h=2), R[:]).then_inc(R_stored, 16)
            sp.dma_start(table[:], ffn_w.partition_broadcast(P)).then_inc(ffn_in, 16)
            for w in range(O_0, PIECES):
                load_piece(TILES, w)
            store_y(TILES - 1, y_prompt[(TILES - 1) * P:TILES * P, :], P)
            store_y(TILES, y_sample, ST)
            sp.wait_ge(y_stored, 16 * (TILES + 1))
            sp.wait_ge(lat_stored, 32 * (TILES + 1))
            sp.wait_ge(s_R_stored, 16 * 32)
            sp.wait_ge(R_stored, 16)

        @block.gpsimd
        def _(pool):
            pool.iota(iota16[:], [[1, K]], channel_multiplier=0, allow_small_or_imprecise_dtypes=True).then_inc(const_set, 1)

            def gathers(t, n):
                pool.wait_ge(handed, t + 1)
                for k in range(SLOTS):
                    pool.wait_ge(row_free, t * SLOTS + k + 1)
                    apart(pool)
                    pool.indirect_dma_start(
                        out=ring[0:n, k % RING, :], out_offset=None, in_=experts,
                        in_offset=bass.IndirectOffsetOnAxis(ap=codes[0:n, k:k + 1], axis=0),
                    ).then_inc(row_in[k % RING], 16)

            gathers(0, P)
            with pool.Fori(1, TILES) as i:
                gathers(i, P)
            gathers(TILES, ST)

        @block.tensor
        def _(pe):
            def expert_slots(t, k0, k1, n):
                for k in range(k0, k1):
                    pe.wait_ge(diag_ready, t * SLOTS + k + 1)
                    if k == 0 and not (isinstance(t, int) and t == 0):
                        pe.wait_ge(y_ready, t)
                    for c in range(2):
                        mm = pe.matmul(acc[0:n, c, :], diag[0:n, k % DIAGS, 0:n],
                                       ring[0:n, k % RING, D + c * 512:D + (c + 1) * 512],
                                       start=(k == 0), stop=(k == SLOTS - 1))
                    mm.then_inc(row_free, 1)

            def turn(t, j, src, n):
                pe.wait_ge(wide_ready, 3 * t + j + 1)
                for c in range(DC):
                    mm = pe.transpose(ps[:, 2 + c // 4, (c % 4) * P:(c % 4) * P + n],
                                      src[0:n, c * P:(c + 1) * P], ident[0:n, 0:n])
                mm.then_inc(turned, 1)

            def xT_copied(t, j):
                pe.wait_ge(xT_a, 3 * t + j + 1)
                pe.wait_ge(xT_b, 3 * t + j + 1)

            def piece(t, w, out, n, cols=PIECE):
                if w in (0, O_0):
                    xT_copied(t, 0 if w == 0 else 1)
                pe.wait_ge(w_in_buf[w % 2], 16 * ((PIECES // 2) * t + w // 2 + 1))
                for c in range(DC):
                    mm = pe.matmul(out, xT[:, c, 0:n], wbuf[:, w % 2, c, 0:cols], start=(c == 0), stop=(c == DC - 1))
                mm.then_inc(piece_done, 1)

            IN_BANK = (2, 2, 3, 3, 4, 4, 5, 5, 0, 0)

            def project(t, w, n):
                cols = LAT - PIECE if w == 1 else PIECE
                piece(t, w, ps[0:n, 2 + IN_BANK[w], (w % 2) * PIECE:(w % 2) * PIECE + cols], n, cols)

            def latents(t, n):
                pe.wait_ge(lat_ready, t + 1)
                for c in range(3):
                    mm = pe.transpose(ps[:, 3, c * P:c * P + n], latn[0:n, c * P:(c + 1) * P], ident[0:n, 0:n])
                mm.then_inc(latT_ps, 1)

            def weights_landed(t, w):
                pe.wait_ge(w_in_buf[w % 2], 16 * ((PIECES // 2) * t + w // 2 + 1))

            def queries(t, n):
                pe.wait_ge(latT_ready, t + 1)
                weights_landed(t, N_IN)
                for g, b in ((0, 2), (1, 1)):
                    for c in range(2):
                        mm = pe.matmul(bank(b, n, 384), latT[:, c, 0:n], uq[:, c, g * 384:(g + 1) * 384],
                                       start=(c == 0), stop=(c == 1))
                mm.then_inc(piece_done, 1)
                weights_landed(t, N_IN + 1)

            def qkv(t, slots):
                queries(t, P)
                pe.matmul(bank(3), latT[:, 2, :], uk, start=True, stop=True)
                pe.matmul(bank(4), latT[:, 2, :], uv, start=True, stop=True).then_inc(piece_done, 1)
                slots()
                slots()
                pe.wait_ge(qk_ready, t + 1)
                pe.wait_ge(rg_ready, t + 1)
                for h in range(H):
                    mm = pe.transpose(ps[0:QK, 2 + (0, 5)[h // 4], (h % 4) * P:(h % 4 + 1) * P], qbuf[:, h, :], ident[:])
                mm.then_inc(qT_ps, 1)
                for h in range(H):
                    mm = pe.transpose(ps[0:QK, 2 + (1, 2)[h // 4], (h % 4) * P:(h % 4 + 1) * P], kbuf[:, h, :], ident[:])
                mm.then_inc(kT_ps, 1)

            def retention_turn(t, n):
                for src, b in ((rq, 3), (rk, 4)):
                    for r in range(4):
                        mm = pe.transpose(ps[:, 2 + b, r * P:r * P + n], src[0:n, r * P:(r + 1) * P], ident[0:n, 0:n])
                mm.then_inc(rT_ps, 1)

            def retention_inner(t, n):
                pe.wait_ge(rT_ready, t + 1)
                for h in range(H):
                    a = 64 * (h % 2)
                    mm = pe.matmul(ps[0:n, 2 + (0, 5)[h % 2], (h // 2) * P:(h // 2) * P + n],
                                   rkT[a:a + 64, h // 2, 0:n], rqT[a:a + 64, h // 2, 0:n], start=True, stop=True)
                mm.then_inc(inner_ps, 1)

            def retention_out(t, n):
                pe.wait_ge(inner_ready, t + 1)
                for h in range(H):
                    mm = pe.matmul(ps[0:n, 3, h * 64:(h + 1) * 64], inT[0:n, h, 0:n], rv[0:n, h * 64:(h + 1) * 64],
                                   start=True, stop=True)
                mm.then_inc(o_ps, 1)

            def retention(t, slots):
                pe.wait_ge(v_ready, t + 1)
                retention_turn(t, P)
                slots()
                pe.wait_ge(qT_ready, t + 1)
                retention_inner(t, P)
                pe.wait_ge(kT_ready, t + 1)
                pe.wait_ge(R_ready, t + 1)
                for h in range(H):
                    a = 64 * (h % 2)
                    pe.matmul(ps[:, 4 + h % 2, (h // 2) * 64:(h // 2 + 1) * 64], rqT[a:a + 64, h // 2, :], R[a:a + 64, h // 2, :],
                              start=True, stop=True)
                for h in range(H):
                    a = 64 * (h % 2)
                    mm = pe.matmul(ps[a:a + 64, 6, (h // 2) * 64:(h // 2 + 1) * 64], kd[:, h * 64:(h + 1) * 64],
                                   rv[:, h * 64:(h + 1) * 64], start=True, stop=True)
                mm.then_inc(cross_ps, 1)
                slots()
                retention_out(t, P)
                slots()

            def attention(t, s):
                if s < H:
                    if s == 0:
                        pe.wait_ge(o_taken, t + 1)
                    else:
                        pe.wait_ge(scores_ready, H * t + s)
                    for c in range(2):
                        mm = pe.matmul(bank(c), qT[0:QK, s, :], kT[0:QK, s, c * 512:(c + 1) * 512], start=True, stop=True)
                    mm.then_inc(scores_ps, 1)
                if 1 <= s <= H:
                    pe.wait_ge(prob_ready, H * t + s)
                    if s >= 2:
                        pe.wait_ge(probT_a, H * t + s - 1)
                        pe.wait_ge(probT_b, H * t + s - 1)
                    for j in range(TILES):
                        mm = pe.transpose(ps[:, 4 + j // 4, (j % 4) * P:(j % 4 + 1) * P],
                                          scores[:, (s - 1) % 2, j * P:(j + 1) * P], ident[:])
                    mm.then_inc(probT_ps, 1)
                if s >= 2:
                    h = s - 2
                    pe.wait_ge(probT_a, H * t + h + 1)
                    pe.wait_ge(probT_b, H * t + h + 1)
                    for j in range(TILES):
                        mm = pe.matmul(ps[:, 6, h * 64:(h + 1) * 64], probT[:, h % 2, j * P:(j + 1) * P],
                                       vN[:, j, h * 64:(h + 1) * 64], start=(j == 0), stop=(j == TILES - 1))
                    mm.then_inc(pv_ps, 1)

            def out(t, n, slots):
                turn(t, 1, mix, n)
                slots()
                for w in range(N_O):
                    if w == 2:
                        slots()
                    piece(t, O_0 + w, ps[0:n, 4 + w // 2, (w % 2) * PIECE:(w % 2 + 1) * PIECE], n)

            def peer(t, s, n, slots):
                if s == 0:
                    xT_copied(t, 2)
                w = PQ_0 + s
                for j in range(2):
                    if s < H:
                        if j == 0:
                            weights_landed(t, w)
                        for c in range(DC):
                            mm = pe.matmul(ps[:, 4 + s % 2, j * P:j * P + n], wbuf[:, w % 2, c, j * P:(j + 1) * P],
                                           xT[:, c, 0:n], start=(c == 0), stop=(c == DC - 1))
                        if j == 1:
                            mm.then_inc(piece_done, 1)
                    if j == 0 and s >= 1:
                        h = s - 1
                        pe.wait_ge(pq_ready, H * t + h + 1)
                        if h >= 2:
                            pe.wait_ge(keys_copied, H * t + h - 1)
                        for a, kk in enumerate((k1T, k2T)):
                            mm = pe.matmul(ps[0:n, 6 + h % 2, a * P:(a + 1) * P], pq[:, h % 2, a * P:a * P + n], kk[:],
                                           start=True, stop=True)
                        mm.then_inc(keys_ps, 1)
                    slots()
                slots()

            def prompt_front(t, slots):
                slots()
                turn(t, 0, mix, P)
                slots()
                for w in range(N_IN):
                    project(t, w, P)
                    slots()
                slots()
                latents(t, P)
                slots()
                qkv(t, slots)
                slots()
                retention(t, slots)
                slots()
                slots()
                for s in range(H + 2):
                    attention(t, s)
                    slots()
                out(t, P, slots)
                slots()
                slots()
                turn(t, 2, xn_next, P)
                slots()
                for s in range(H + 1):
                    peer(t, s, P, slots)
                slots()

            def sample_sequence(b):
                pe.wait_ge(pages_in[b % 2], 16 * 2 * PAGES * (b // 2 + 1))
                pe.wait_ge(kp2_ready, b + 1)
                if b:
                    pe.wait_ge(s_oT, b)
                for j in range(PAGES):
                    pe.transpose(ps[:, 2 + j // 4, (j % 4) * P:(j % 4 + 1) * P], pg[:, b % 2, j, 0:KVR], ident[:])
                for j in range(PAGES):
                    mm = pe.transpose(ps[0:64, 4 + j // 4, (j % 4) * P:(j % 4 + 1) * P], kp2[:, j, :], ident[:])
                mm.then_inc(pageT_ps, 1)
                pe.wait_ge(cT_ready, b + 1)
                pe.wait_ge(kpT_ready, b + 1)
                for j in range(PAGES + 1):
                    m = (PAGES + 1) * b + j
                    if m >= 2:
                        pe.wait_ge(kn_sq, m - 1)
                    lhs = cT[:, j * P:(j + 1) * P] if j < PAGES else latT[:, 2, b * STEPS:(b + 1) * STEPS]
                    n = P if j < PAGES else STEPS
                    pe.matmul(ps[0:n, 6 + m % 2, :], lhs, uk, start=True, stop=True).then_inc(kn_ps, 1)
                for j in range(PAGES + 1):
                    n = P if j < PAGES else STEPS
                    c = cT[:, j * P:(j + 1) * P] if j < PAGES else latT[:, 2, b * STEPS:(b + 1) * STEPS]
                    k = kpT[:, j * P:(j + 1) * P] if j < PAGES else kpTn[:, b * STEPS:(b + 1) * STEPS]
                    q = QT[:, b].rearrange("p h s -> p (h s)")
                    qr = QPT[:, b].rearrange("p h s -> p (h s)")
                    pe.matmul(ps[0:n, 2, j * 32:(j + 1) * 32], c, q, start=True, stop=False)
                    pe.matmul(ps[0:n, 2, j * 32:(j + 1) * 32], k[0:32], qr[0:32], start=False, stop=True)
                for j in range(PAGES + 1):
                    n = P if j < PAGES else STEPS
                    k = kpT[:, j * P:(j + 1) * P] if j < PAGES else kpTn[:, b * STEPS:(b + 1) * STEPS]
                    mm = pe.matmul(ps[0:n, 3, j * 8:(j + 1) * 8], k[32:64], ones32[32:64], start=True, stop=True)
                mm.then_inc(sT_ps, 1)
                pe.wait_ge(sT_ready, b + 1)
                for j in range(PAGES):
                    pe.transpose(ps[0:32, 4 + j // 4, (j % 4) * P:(j % 4 + 1) * P], sT[:, j * 32:(j + 1) * 32], ident[:])
                pe.wait_ge(kn_sq, (PAGES + 1) * (b + 1))
                pe.transpose(ps[0:32, 6, 0:STEPS], sT[0:STEPS, 256:288], ident[0:STEPS, 0:STEPS]).then_inc(s_ps, 1)
                pe.wait_ge(s_prob, b + 1)
                for j in range(PAGES):
                    pe.transpose(ps[:, 2, j * 32:(j + 1) * 32], prob[0:32, j * P:(j + 1) * P], ident[0:32, 0:32])
                pe.transpose(ps[0:STEPS, 2, 256:288], prob[0:32, 1024:1028], ident[0:32, 0:32]).then_inc(s_pT_ps, 1)
                pe.wait_ge(s_pT, b + 1)
                if b == 0:
                    pe.wait_ge(s_cnew_in, 16 * SEQS)
                for j in range(PAGES):
                    pe.matmul(ps[0:32, 3, 0:KVR], pT[:, j * 32:(j + 1) * 32], pg[:, b % 2, j, 0:KVR],
                              start=(j == 0), stop=False)
                pe.matmul(ps[0:32, 3, 0:KVR], pT[0:STEPS, 256:288], cnew[:, b, :], start=False, stop=True).then_inc(s_o_ps, 1)
                pe.wait_ge(s_o, b + 1)
                pe.transpose(ps[:, 4, 0:32], ol[0:32, :], ident[0:32, 0:32]).then_inc(s_oT_ps, 1)

            def sample_front(slots):
                t, n = TILES, ST
                slots()
                turn(t, 0, mix, n)
                slots()
                for w in range(N_IN):
                    project(t, w, n)
                    slots()
                slots()
                latents(t, n)
                slots()
                queries(t, n)
                pe.wait_ge(rg_ready, t + 1)
                pe.wait_ge(s_q_ready, 1)
                for r in range(4):
                    pe.transpose(ps[:, 2, r * 32:(r + 1) * 32], mix[0:n, r * P:(r + 1) * P], ident[0:n, 0:n])
                for h in range(H):
                    pe.transpose(ps[0:32, 3, h * 32:(h + 1) * 32], qp[0:n, h * 32:(h + 1) * 32], ident[0:n, 0:n])
                pe.transpose(ps[0:64, 4, 0:32], kp2n[0:n, :], ident[0:n, 0:n]).then_inc(s_q_ps, 1)
                pe.wait_ge(s_q_copied, 1)
                for h in range(H):
                    a = 64 * (h % 2)
                    mm = pe.matmul(ps[:, 4 + h % 2, (h // 2) * 32:(h // 2 + 1) * 32], wkT[a:a + 64, h // 2, :], qnT[a:a + 64, h // 2, :],
                                   start=True, stop=True)
                mm.then_inc(s_ql_ps, 1)
                slots()
                retention_turn(t, n)
                retention_inner(t, n)
                pe.wait_ge(s_ql_ready, 1)
                for h in range(H):
                    a = 64 * (h % 2)
                    if h >= 2:
                        pe.wait_ge(s_cross_taken, h - 1)
                    else:
                        pe.wait_ge(s_state_in, 16 * 32)
                    pe.matmul(ps[0:n, 4 + h % 2, :], rqT[a:a + 64, h // 2, 0:n],
                              Rs[a:a + 64, h // 2].rearrange("p b v -> p (b v)"), start=True, stop=True).then_inc(s_cross_ps, 1)
                retention_out(t, n)
                for h in range(H):
                    pe.wait_ge(s_vexp, h + 1)
                    a = 64 * (h % 2)
                    if h == 0:
                        pe.wait_ge(inner_ready, t + 1)
                    if h >= 2 and h % 2 == 0:
                        pe.wait_ge(s_R_ready, h // 2)
                    pe.matmul(ps[a:a + 64, 7, :], kd[0:n, h * 64:(h + 1) * 64],
                              mix[0:n, (h % 2) * 512:(h % 2 + 1) * 512], start=True, stop=True).then_inc(s_R_ps, 1)
                pe.wait_ge(o_taken, t + 1)
                slots()
                for b in range(SEQS):
                    sample_sequence(b)
                    slots()
                pe.wait_ge(s_oT, SEQS)
                for h in range(H):
                    mm = pe.matmul(ps[0:n, 2, h * 64:(h + 1) * 64], OL[:, h].rearrange("p b s -> p (b s)"),
                                   uv[:, h * 64:(h + 1) * 64], start=True, stop=True)
                mm.then_inc(piece_done, 1)
                out(t, n, slots)
                slots()
                slots()
                turn(t, 2, xn_next, n)
                slots()
                for s in range(H + 1):
                    peer(t, s, n, slots)
                slots()

            pe.sem_inc(row_free, RING)
            pe.wait_ge(const_in, 16 * N_CONST)
            prompt_front(0, lambda: None)
            with pe.Fori(1, TILES) as i:
                between = Between(expert_slots, i - 1, prompt_slots(), P, behind=True)
                prompt_front(i, between)
                between.rest()
            between = Between(expert_slots, TILES - 1, sample_slots(), P, behind=True)
            sample_front(between)
            between.rest()
            expert_slots(TILES, 0, SLOTS, ST)

        @block.scalar
        def _(act):
            own = Steps(act, act_s)

            def make_diags(t, k, n):
                act.wait_ge(coef_done, t * (SLOTS // 2) + k // 2 + 1)
                for j in range(k, k + 2):
                    act.wait_ge(row_free, t * SLOTS + j + 1 + RING - DIAGS)
                    act.activation(diag[0:n, j % DIAGS, 0:n], ident[0:n, 0:n], ACT.Copy,
                                   scale=coefs[0:n, j:j + 1]).then_inc(diag_ready, 1)

            def expert_slots(t, k0, k1, n):
                for k in range(k0, k1, 2):
                    if k:
                        make_diags(t, k - 2, n)
                    act.wait_ge(dot_done, t * SLOTS + k + 2)
                    act.activation(gelus[0:n, k:k + 2], dots[0:n, k:k + 2], ACT.Gelu).then_inc(gelu_done, 1)

            def turned_copy(t, j, n, scale):
                act.wait_ge(turned, 3 * t + j + 1)
                own.wait()
                if scale is None:
                    src = bank(1).rearrange("p (c q) -> p c q", c=4)[:, :, 0:n]
                    own.raises(act.activation(xT[:, 4:8, 0:n], src, ACT.Copy), xT_b, 3 * t + j + 1)
                else:
                    for c in range(4):
                        ins = act.activation(xT[:, 4 + c, 0:n], bank(1, P, c * P + n)[:, c * P:], ACT.Copy, scale=scale[:, 4 + c:5 + c])
                        if c < 3:
                            own.done(ins)
                    own.raises(ins, xT_b, 3 * t + j + 1)

            def square_sum(src, n, width, at):
                own.wait()
                out = junk if width == D else junk_lat
                return act.activation(out[0:n, 0:width], src, ACT.Square, accum_out=ss[0:n, at:at + 1])

            def norm_in(t, n):
                act.wait_ge(tile_in, 48 * (t + 1))
                own.raises(square_sum(resid[0:n, :], n, D, 0), squares, 4 * t + 1)

            def lat_squares(t, n):
                act.wait_ge(piece_done, PIECES * t + 2)
                if not (isinstance(t, int) and t == 0):
                    act.wait_ge(lat_stored, 32 * t)
                own.wait()
                own.done(act.activation(lat[0:n, :], bank(2, n, LAT), ACT.Copy))
                own.done(square_sum(lat[0:n, 0:QR], n, QR, 1))
                own.done(square_sum(lat[0:n, QR:QR + KVR], n, KVR, 2))
                own.raises(square_sum(lat[0:n, QR + KVR:LAT], n, ROPE, 3), squares, 4 * t + 2)

            def values_and_gates(t, n):
                act.wait_ge(piece_done, PIECES * t + 8)
                own.wait()
                own.done(act.activation(rv[0:n, :], bank(5, n), ACT.Copy))
                act.wait_ge(piece_done, PIECES * t + 10)
                own.done(act.activation(th[0:n, :], bank(0, n), ACT.Tanh, scale=0.5))
                own.raises(act.activation(rg[0:n, :], bank(0, n), ACT.Copy), rg_ready, t + 1)

            def q_squares(t, n):
                if not (isinstance(t, int) and t == 0):
                    act.wait_ge(y_stored, 16 * (t - 1))
                act.wait_ge(piece_done, PIECES * t + N_IN + 1)
                own.wait()
                own.done(act.activation(sqq[0:n, 0:384], bank(2, n, 384), ACT.Square))
                return act.activation(sqq[0:n, 384:768], bank(1, n, 384), ACT.Square)

            def qkv(t, slots):
                own.done(q_squares(t, P))
                act.wait_ge(piece_done, PIECES * t + O_0)
                own.raises(act.activation(sqk, bank(3), ACT.Square), squares, 4 * t + 3)
                own.raises(act.activation(vN[:, bass.ds(t, 1), :].rearrange("p o c -> p (o c)"), bank(4), ACT.Copy), v_ready, t + 1)
                slots()
                slots()
                act.wait_ge(qT_ps, t + 1)
                own.done(act.activation(qT[0:QK, 0:4, :].rearrange("p h q -> p (h q)"), bank(0, QK), ACT.Copy))
                own.raises(act.activation(qT[0:QK, 4:8, :].rearrange("p h q -> p (h q)"), bank(5, QK), ACT.Copy), qT_ready, t + 1)

            def retention(t, n):
                act.wait_ge(rT_ps, t + 1)
                own.wait()
                src = [ps[:, 2 + b, :].rearrange("p (r q) -> p r q", r=4)[:, :, 0:n] for b in (3, 4)]
                own.done(act.activation(rqT[:, :, 0:n], src[0], ACT.Copy))
                own.raises(act.activation(rkT[:, :, 0:n], src[1], ACT.Copy, scale=0.125), rT_ready, t + 1)

            def attention(t, s):
                if s < H:
                    act.wait_ge(scores_ready, H * t + s + 1)
                    own.raises(act.activation(scores[:, s % 2, :], scores[:, s % 2, :], ACT.Exp, bias=nb[:, s:s + 1],
                                              scale=SCALE, accum_out=sums[:, s:s + 1]), prob_ready, H * t + s + 1)
                if 1 <= s <= H:
                    h = s - 1
                    act.wait_ge(probT_ps, H * t + h + 1)
                    if h >= 2:
                        act.wait_ge(pv_ps, H * t + h - 1)
                    own.raises(act.activation(probT[:, h % 2, 512:1024], bank(3), ACT.Copy), probT_b, H * t + h + 1)

            def h_squares(t, n):
                act.wait_ge(h_ready, t + 1)
                own.raises(square_sum(resid[0:n, :], n, D, 0), squares, 4 * t + 4)

            def peer(t, s, n):
                if s < H:
                    act.wait_ge(piece_done, PIECES * t + PQ_0 + s + 1)
                    if s >= 2:
                        act.wait_ge(keys_ps, H * t + s - 1)
                    src = ps[:, 4 + s % 2, 0:256].rearrange("p (j q) -> p j q", j=2)[:, :, 0:n]
                    dst = pq[:, s % 2, :].rearrange("p (j q) -> p j q", j=2)[:, :, 0:n]
                    own.raises(act.activation(dst, src, ACT.Copy), pq_ready, H * t + s + 1)

            def copy_keys(t, s, n):
                if s >= 1:
                    h = s - 1
                    act.wait_ge(keys_ps, H * t + h + 1)
                    if h >= 2:
                        act.wait_ge(keys_used, H * t + h - 1)
                    own.raises(act.activation(sS[0:n, h % 2], ps[0:n, 6 + h % 2, 0:256].rearrange("p (j k) -> p j k", j=2), ACT.Copy),
                               keys_copied, H * t + h + 1)

            def gate_exps(t, n):
                act.wait_ge(gate_in, t + 1)
                own.raises(act.activation(gate_x[0:n], gate_x[0:n], ACT.Exp), gate_exp, t + 1)

            def out_and_peer(t, n, slots):
                turned_copy(t, 1, n, None)
                slots()
                slots()
                slots()
                h_squares(t, n)
                slots()
                turned_copy(t, 2, n, None)
                slots()
                for s in range(H + 1):
                    copy_keys(t, s, n)
                    slots()
                    peer(t, s, n)
                    slots()
                    slots()
                gate_exps(t, n)
                slots()

            def prompt_front(t, slots):
                slots()
                norm_in(t, P)
                turned_copy(t, 0, P, attn_wc)
                slots()
                for w in range(N_IN):
                    if w == 1:
                        lat_squares(t, P)
                    slots()
                values_and_gates(t, P)
                slots()
                slots()
                qkv(t, slots)
                slots()
                slots()
                retention(t, P)
                slots()
                slots()
                slots()
                slots()
                for s in range(H + 2):
                    attention(t, s)
                    slots()
                out_and_peer(t, P, slots)

            def sample_sequence(b):
                act.wait_ge(pageT_ps, b + 1)
                own.wait()
                own.done(act.activation(cT[:, 0:512], bank(0), ACT.Copy))
                own.raises(act.activation(cT[:, 512:1024], bank(1), ACT.Copy), cT_ready, b + 1)
                for j in range(PAGES + 1):
                    m = (PAGES + 1) * b + j
                    n = P if j < PAGES else STEPS
                    act.wait_ge(kn_ps, m + 1)
                    if m >= 2:
                        act.wait_ge(kn_taken, m - 1)
                    own.raises(act.activation(sqn[0:n, m % 2, :], ps[0:n, 6 + m % 2, :], ACT.Square), kn_sq, m + 1)
                act.wait_ge(s_max, b + 1)
                own.done(act.activation(prob[0:32, 0:1024], ps[0:32, 4:6, :].rearrange("p a b -> p (a b)"), ACT.Exp,
                                        bias=smx[0:32, 3:4], scale=SCALE, accum_out=smx[0:32, 4:5]))
                own.raises(act.activation(prob[0:32, 1024:1028], s4[0:32], ACT.Exp, bias=smx[0:32, 3:4], scale=SCALE,
                                          accum_out=smx[0:32, 5:6]), s_prob, b + 1)

            def sample_front(slots):
                t, n = TILES, ST
                slots()
                norm_in(t, n)
                turned_copy(t, 0, n, attn_wc)
                slots()
                for w in range(N_IN):
                    if w == 1:
                        lat_squares(t, n)
                    slots()
                values_and_gates(t, n)
                slots()
                slots()
                own.raises(q_squares(t, n), squares, 4 * t + 3)
                slots()
                retention(t, n)
                slots()
                for b in range(SEQS):
                    sample_sequence(b)
                    slots()
                out_and_peer(t, n, slots)

            prompt_front(0, lambda: None)
            own.close()
            with act.Fori(1, TILES) as i:
                prompt_front(i, Between(expert_slots, i - 1, prompt_slots(), P))
                make_diags(i - 1, SLOTS - 2, P)
                own.close()
            sample_front(Between(expert_slots, TILES - 1, sample_slots(), P))
            make_diags(TILES - 1, SLOTS - 2, P)
            expert_slots(TILES, 0, SLOTS, ST)
            make_diags(TILES, SLOTS - 2, ST)

        @block.vector
        def _(dve):
            own = Steps(dve, vec)

            def do(instruction_of, *args, behind=0, **kwargs):
                own.wait(behind)
                own.done(instruction_of(*args, **kwargs))

            def do_signal(sem_, value, instruction_of, *args, behind=0, **kwargs):
                own.wait(behind)
                own.raises(instruction_of(*args, **kwargs), sem_, value)

            def root(n, w):
                x, y, z = (a[0:n, 0:w] for a in (root_x, root_y, root_t))
                do(dve.tensor_scalar, y.bitcast(I32), x.bitcast(I32), 1, None, ALU.logical_shift_right)
                do(dve.tensor_scalar, y.bitcast(I32), y.bitcast(I32), -1.0, float(0x5f3759df), ALU.mult, ALU.add)
                for _ in range(3):
                    do(dve.tensor_tensor, z, y, y, ALU.mult)
                    do(dve.scalar_tensor_tensor, out=z, in0=z, scalar=-0.5, in1=x, op0=ALU.mult, op1=ALU.mult)
                    do(dve.scalar_tensor_tensor, out=y, in0=z, scalar=1.5, in1=y, op0=ALU.add, op1=ALU.mult)

            def make_coefs(t, k, n):
                dve.wait_ge(gelu_done, t * (SLOTS // 2) + k // 2 + 1)
                dve.tensor_tensor(coefs[0:n, k:k + 2], gelus[0:n, k:k + 2], gates[0:n, k:k + 2], ALU.mult).then_inc(coef_done, 1)

            def expert_slots(t, k0, k1, n):
                for k in range(k0, k1):
                    if k % 2 == 1 and k > 1:
                        make_coefs(t, k - 3, n)
                    dve.wait_ge(row_in[k % RING], 16 * ((SLOTS // RING) * t + k // RING + 1))
                    apart(dve)
                    u = ring[0:n, k % RING, 0:D]
                    dve.tensor_tensor_reduce(u, u, xn_cur[0:n], 1.0, 0.0, ALU.mult, ALU.add,
                                             dots[0:n, k:k + 1]).then_inc(dot_done, 1)

            def hand_numbers(t, n):
                do_signal(handed, t + 1, dve.tensor_copy, codes[0:n], codes_next[0:n])

            def hand_rows(t, n):
                if not (isinstance(t, int) and t == 0):
                    dve.wait_ge(dot_done, SLOTS * t)
                    dve.wait_ge(coef_done, (SLOTS // 2) * t)
                do(dve.tensor_copy, xn_cur[0:n], xn_next[0:n])
                do(dve.tensor_copy, gates[0:n], gates_next[0:n], behind=1)

            def hand_h(t, n):
                do_signal(h_moved, t + 1, dve.tensor_copy, h_cur[0:n], resid[0:n])

            def finish(t, n):
                if not (isinstance(t, int) and t == 0):
                    dve.wait_ge(y_stored, 16 * t)
                dve.wait_ge(row_free, SLOTS * (t + 1) + RING)
                do_signal(y_ready, t + 1, dve.tensor_tensor, ybuf[0:n], h_cur[0:n],
                          acc[0:n].rearrange("p a b -> p (a b)"), ALU.add)

            def turned_copy(t, j, n, scale):
                dve.wait_ge(turned, 3 * t + j + 1)
                src, dst = bank(0).rearrange("p (c q) -> p c q", c=4)[:, :, 0:n], xT[:, 0:4, 0:n]
                if scale is None:
                    do_signal(xT_a, 3 * t + j + 1, dve.tensor_copy, dst, src)
                else:
                    do_signal(xT_a, 3 * t + j + 1, dve.tensor_tensor, dst, src, over(scale[:, 0:4], 2, [P, 4, n]), ALU.mult)

            def norm_in(t, n):
                dve.wait_ge(squares, 4 * t + 1)
                do(dve.tensor_scalar, root_x[0:n, 0:1], ss[0:n, 0:1], 1.0 / D, EPS, ALU.mult, ALU.add)
                root(n, 1)
                do_signal(wide_ready, 3 * t + 1, dve.tensor_scalar, mix[0:n], resid[0:n], root_y[0:n, 0:1], None, ALU.mult)

            def rotate(dst, src, cos, sin, tmp, shape):
                half = shape[-1] // 2
                do(dve.tensor_tensor, tmp, src, cos, ALU.mult)
                do(dve.tensor_tensor, dst[:, :, 0:half], src[:, :, half:], sin[:, :, 0:half], ALU.mult, behind=1)
                do(dve.tensor_tensor, dst[:, :, half:], src[:, :, 0:half], sin[:, :, half:], ALU.mult, behind=2)
                do(dve.tensor_tensor, dst, dst, tmp, ALU.add)

            def heads(ap, d=64):
                return ap.rearrange("p (h d) -> p h d", d=d)

            def half(ap, a):
                return ap.rearrange("p (r a) d -> p a r d", a=2)[:, a]

            def rotate_retention(t, n, w, b, dst):
                dve.wait_ge(piece_done, PIECES * t + w)
                rotate(heads(dst[0:n]), heads(bank(b, n)), over(rope_t[0:n, 64:128], 1, [n, H, 64]),
                       over(rope_t[0:n, 128:192], 1, [n, H, 64]), heads(ropet[0:n]), [n, H, 64])

            def latents(t, n):
                dve.wait_ge(squares, 4 * t + 2)
                do(dve.tensor_scalar, root_x[0:n, 0:1], ss[0:n, 1:2], 1.0 / QR, EPS, ALU.mult, ALU.add)
                do(dve.tensor_scalar, root_x[0:n, 1:2], ss[0:n, 2:3], 1.0 / KVR, EPS, ALU.mult, ALU.add)
                root(n, 2)
                if not (isinstance(t, int) and t == 0):
                    dve.wait_ge(lat_stored, 32 * t)
                do(dve.tensor_scalar, latn[0:n, 0:QR], lat[0:n, 0:QR], root_y[0:n, 0:1], None, ALU.mult)
                do_signal(lat_ready, t + 1, dve.scalar_tensor_tensor, out=latn[0:n, QR:], in0=lat[0:n, QR:QR + KVR],
                          scalar=root_y[0:n, 1:2], in1=kva_wb[0:n], op0=ALU.mult, op1=ALU.mult)

            def latents_turned(t, n):
                dve.wait_ge(latT_ps, t + 1)
                src = ps[:, 3, 0:384].rearrange("p (c q) -> p c q", c=3)
                do(dve.tensor_tensor, latT[:, 0:2, 0:n], src[:, 0:2, 0:n], over(qa_wc[:], 2, [P, 2, n]), ALU.mult)
                do_signal(latT_ready, t + 1, dve.tensor_copy, latT[:, 2, 0:n], src[:, 2, 0:n])

            def norm_queries(n):
                for g, b in ((0, 2), (1, 1)):
                    do(dve.tensor_tensor, qbuf[0:n, 4 * g:4 * g + 4], heads(bank(b, n, 384), QK),
                       over(root_y[0:n, 4 * g:4 * g + 4], 2, [n, 4, QK]), ALU.mult)
                do(dve.tensor_tensor, qbuf[0:n], qbuf[0:n], over(q_wb[0:n], 1, [n, H, QK]), ALU.mult)
                pe_part = heads(sqq[0:n, 0:256], ROPE)
                do(dve.tensor_copy, pe_part, qbuf[0:n, :, NOPE:])
                rotate(qbuf[0:n, :, NOPE:], pe_part, over(rope_t[0:n, 0:32], 1, [n, H, 32]),
                       over(rope_t[0:n, 32:64], 1, [n, H, 32]), heads(sqq[0:n, 256:512], ROPE), [n, H, 32])

            def rotated_key(dst, n):
                do(dve.tensor_tensor, kpw[0:n], lat[0:n, QR + KVR:], k_wb[0:n, NOPE:], ALU.mult)
                rotate(dst.unsqueeze(1), kpw[0:n].unsqueeze(1), rope_t[0:n, 0:32].unsqueeze(1),
                       rope_t[0:n, 32:64].unsqueeze(1), ropet[0:n, 0:32].unsqueeze(1), [n, 1, 32])

            def qkv(t, slots):
                if not (isinstance(t, int) and t == 0):
                    dve.wait_ge(y_stored, 16 * (t - 1))
                do(dve.tensor_tensor, heads(kd), heads(rk[:]), over(dec_k[:], 2, [P, H, 64]), ALU.mult)
                dve.wait_ge(squares, 4 * t + 3)
                do(dve.tensor_reduce, ms8[:, 0:8], heads(sqq, QK), AX_X, ALU.add)
                do(dve.tensor_reduce, ms8[:, 8:16], heads(sqk), AX_X, ALU.add)
                do(dve.tensor_scalar, ms8[:, 8:16], ms8[:, 8:16], ss[:, 3:4], None, ALU.add)
                do(dve.tensor_scalar, root_x[:, 0:16], ms8[:], 1.0 / QK, EPS, ALU.mult, ALU.add)
                root(P, 16)
                slots()
                norm_queries(P)
                slots()
                rk_ = root_y[:, 8:16]
                do(dve.tensor_tensor, kbuf[:, :, 0:NOPE], heads(bank(3)), over(rk_, 2, [P, H, NOPE]), ALU.mult)
                do(dve.tensor_tensor, kbuf[:, :, 0:NOPE], kbuf[:, :, 0:NOPE], over(k_wb[:, 0:NOPE], 1, [P, H, NOPE]), ALU.mult)
                rotated_key(kpr, P)
                do_signal(qk_ready, t + 1, dve.tensor_tensor, kbuf[:, :, NOPE:], over(kpr, 1, [P, H, ROPE]),
                          over(rk_, 2, [P, H, ROPE]), ALU.mult)
                dve.wait_ge(kT_ps, t + 1)
                slots()
                do(dve.tensor_copy, kT[0:QK, 0:4, bass.ds(t * P, P)], heads(bank(1, QK), P))
                do_signal(kT_ready, t + 1, dve.tensor_copy, kT[0:QK, 4:8, bass.ds(t * P, P)], heads(bank(2, QK), P))

            def group_norm(n, slots):
                o3 = heads(oret[0:n])
                do(dve.tensor_reduce, ms8[0:n, 0:8], o3, AX_X, ALU.add)
                do(dve.tensor_scalar, ms8[0:n, 0:8], ms8[0:n, 0:8], -1.0 / 64, None, ALU.mult)
                do(dve.tensor_tensor, o3, o3, over(ms8[0:n, 0:8], 2, [n, H, 64]), ALU.add)
                do(dve.tensor_tensor, osq[0:n], oret[0:n], oret[0:n], ALU.mult)
                do(dve.tensor_reduce, ms8[0:n, 0:8], heads(osq[0:n]), AX_X, ALU.add)
                do(dve.tensor_scalar, root_x[0:n, 0:8], ms8[0:n, 0:8], 1.0 / 64, EPS, ALU.mult, ALU.add)
                root(n, 8)
                slots()
                do(dve.tensor_tensor, o3, o3, over(root_y[0:n, 0:8], 2, [n, H, 64]), ALU.mult)
                do(dve.tensor_tensor, oret[0:n], oret[0:n], ret_wb[0:n], ALU.mult)
                do(dve.scalar_tensor_tensor, out=th[0:n], in0=th[0:n], scalar=1.0, in1=rg[0:n], op0=ALU.add, op1=ALU.mult)
                do(dve.tensor_tensor, mix[0:n, 512:], oret[0:n], th[0:n], ALU.mult)

            def retention(t, slots):
                dve.wait_ge(inner_ps, t + 1)
                do(dve.tensor_tensor, half(inT, 0), heads(bank(0), P), half(dec_in, 0), ALU.mult)
                do_signal(inner_ready, t + 1, dve.tensor_tensor, half(inT, 1), heads(bank(5), P), half(dec_in, 1), ALU.mult)
                slots()
                dve.wait_ge(cross_ps, t + 1)
                for a in range(2):
                    do(dve.tensor_tensor, half(heads(crossv), a), heads(bank(2 + a, P, 256)),
                       over(dec_cross[:].rearrange("p (r a) -> p a r", a=2)[:, a], 2, [P, 4, 64]), ALU.mult)
                do(dve.tensor_tensor, R[:], R[:], over(dec_state[:], 2, [P, 4, 64]), ALU.mult)
                do_signal(R_ready, t + 2, dve.tensor_tensor, R[:], R[:], heads(bank(4, P, 256)), ALU.add)
                slots()
                dve.wait_ge(o_ps, t + 1)
                do_signal(o_taken, t + 1, dve.tensor_tensor, oret, bank(1), crossv, ALU.add)
                group_norm(P, slots)

            def attention(t, s):
                if s == 0:
                    dve.wait_ge(mask_in, 16 * (t + 1))
                if s < H:
                    dve.wait_ge(scores_ps, H * t + s + 1)
                    own.wait()
                    apart(dve)
                    own.done(dve.tensor_tensor_reduce(scores[:, s % 2, :], ps[:, 2:4, :].rearrange("p a b -> p (a b)"), table[:],
                       1.0, LOWEST, ALU.add, ALU.max, mx[:, s:s + 1]))
                    do_signal(scores_ready, H * t + s + 1, dve.tensor_scalar, nb[:, s:s + 1], mx[:, s:s + 1], -SCALE, None, ALU.mult)
                if 1 <= s <= H:
                    h = s - 1
                    dve.wait_ge(probT_ps, H * t + h + 1)
                    if h >= 2:
                        dve.wait_ge(pv_ps, H * t + h - 1)
                    do_signal(probT_a, H * t + h + 1, dve.tensor_copy, probT[:, h % 2, 0:512], bank(2))
                if s == H + 1:
                    dve.wait_ge(pv_ps, H * (t + 1))
                    do(dve.reciprocal, sums[:], sums[:])
                    do_signal(wide_ready, 3 * t + 2, dve.tensor_tensor, heads(mix[:, 0:512]), heads(bank(4)),
                              over(sums[:], 2, [P, H, 64]), ALU.mult)

            def out(t, n):
                dve.wait_ge(piece_done, PIECES * t + O_0 + 2)
                do(dve.tensor_tensor, resid[0:n, 0:512], resid[0:n, 0:512], bank(2, n), ALU.add)
                dve.wait_ge(piece_done, PIECES * t + O_0 + 4)
                do_signal(h_ready, t + 1, dve.tensor_tensor, resid[0:n, 512:], resid[0:n, 512:], bank(3, n), ALU.add)

            def norm_ffn(t, n):
                dve.wait_ge(squares, 4 * t + 4)
                do(dve.tensor_scalar, root_x[0:n, 0:1], ss[0:n, 0:1], 1.0 / D, EPS, ALU.mult, ALU.add)
                root(n, 1)
                dve.wait_ge(ffn_in, 16 * (t + 1))
                do_signal(wide_ready, 3 * t + 3, dve.scalar_tensor_tensor, out=xn_next[0:n], in0=resid[0:n],
                          scalar=root_y[0:n, 0:1], in1=table[0:n], op0=ALU.mult, op1=ALU.mult)

            def top16(sets):
                b = len(sets) - 1
                for values, indices, src, copy in sets:
                    do(dve.max, values[:, 0:8], src, behind=b)
                for values, indices, src, copy in sets:
                    do(dve.max_index, indices[:, 0:8], values[:, 0:8], src, behind=b)
                for values, indices, src, copy in sets:
                    do(dve.match_replace, copy, values[:, 0:8], src, LOWEST, behind=b)
                for values, indices, src, copy in sets:
                    do(dve.max, values[:, 8:16], copy, behind=b)
                for values, indices, src, copy in sets:
                    do(dve.max_index, indices[:, 8:16], values[:, 8:16], copy, behind=b)

            def peer(t, s, n, slots):
                if s == 0:
                    slots()
                    slots()
                    slots()
                    return
                h = s - 1
                slots()
                dve.wait_ge(keys_copied, H * t + h + 1)
                own.wait()
                own.done(dve.tensor_scalar(passing[0:n], iota16[0:n, 0:1], 0.0, None, ALU.add))
                top16([(vals[0:n, j], idx8[0:n, j], sS[0:n, h % 2, j], sS2[0:n, j]) for j in range(2)])
                slots()
                do_signal(keys_used, H * t + h + 1, dve.tensor_tensor, cand[0:n].rearrange("p (a b) -> p a b", a=K),
                          over(vals[0:n, 0], 2, [n, K, K]), over(vals[0:n, 1], 1, [n, K, K]), ALU.add)
                own.wait()
                own.done(dve.tensor_scalar(passing[0:n], iota16[0:n, 0:1], 0.0, None, ALU.add))
                top16([(top_v[0:n, h], top_c[0:n], cand[0:n], cand2[0:n])])
                slots()
                do(dve.tensor_scalar, ab[0:n, 0], top_c[0:n], 4, None, ALU.logical_shift_right)
                do(dve.tensor_scalar, ab[0:n, 1], top_c[0:n], K - 1, None, ALU.bitwise_and, behind=1)
                for j in range(2):
                    do(dve.tensor_tensor, hot[0:n, j], over(iota16[0:n], 1, [n, K, K]), over(ab[0:n, j], 2, [n, K, K]), ALU.is_equal, behind=1)
                for j in range(2):
                    do(dve.tensor_tensor, hot[0:n, j], hot[0:n, j], over(idx8[0:n, j], 1, [n, K, K]), ALU.mult, behind=1)
                for j in range(2):
                    do(dve.tensor_reduce, e12[0:n, j], hot[0:n, j], AX_X, ALU.add, behind=1)
                do(dve.scalar_tensor_tensor, out=codes_next[0:n, h * K:(h + 1) * K], in0=e12[0:n, 0], scalar=128.0,
                   in1=e12[0:n, 1], op0=ALU.mult, op1=ALU.add)

            def gate_logits(t, n):
                do_signal(gate_in, t + 1, dve.tensor_tensor, gate_x[0:n], top_v[0:n],
                          top_v[0:n, :, 0:1].to_broadcast([n, H, K]), ALU.subtract)
                dve.wait_ge(gate_exp, t + 1)
                do(dve.tensor_reduce, ms8[0:n, 0:8], gate_x[0:n], AX_X, ALU.add)
                do(dve.reciprocal, ms8[0:n, 0:8], ms8[0:n, 0:8])
                do(dve.tensor_tensor, gates_next[0:n].rearrange("p (h k) -> p h k", h=H), gate_x[0:n],
                   over(ms8[0:n, 0:8], 2, [n, H, K]), ALU.mult)

            def out_and_peer(t, n, slots):
                turned_copy(t, 1, n, None)
                slots()
                slots()
                out(t, n)
                slots()
                norm_ffn(t, n)
                slots()
                turned_copy(t, 2, n, None)
                slots()
                for s in range(H + 1):
                    peer(t, s, n, slots)
                gate_logits(t, n)
                slots()

            def project(t, n, slots):
                slots()
                norm_in(t, n)
                turned_copy(t, 0, n, attn_wc)
                slots()
                for w in range(N_IN):
                    if w == 4:
                        rotate_retention(t, n, 4, 3, rq)
                    if w == 6:
                        rotate_retention(t, n, 6, 4, rk)
                    slots()
                latents(t, n)
                slots()
                latents_turned(t, n)
                slots()

            def prompt_front(t, slots):
                project(t, P, slots)
                qkv(t, slots)
                slots()
                retention(t, slots)
                slots()
                for s in range(H + 2):
                    attention(t, s)
                    slots()
                out_and_peer(t, P, slots)

            def sample_queries():
                t, n = TILES, ST
                do(dve.tensor_tensor, heads(kd[0:n]), heads(rk[0:n]), over(dec_k_s[0:n], 2, [n, H, 64]), ALU.mult)
                dve.wait_ge(squares, 4 * t + 3)
                do(dve.tensor_reduce, ms8[0:n, 0:8], heads(sqq[0:n], QK), AX_X, ALU.add)
                do(dve.tensor_scalar, root_x[0:n, 0:8], ms8[0:n, 0:8], 1.0 / QK, EPS, ALU.mult, ALU.add)
                root(n, 8)
                norm_queries(n)
                do(dve.tensor_tensor, heads(mix[0:n, 0:512]), qbuf[0:n, :, 0:NOPE], over(k_wb[0:n, 0:NOPE], 1, [n, H, NOPE]), ALU.mult)
                do(dve.tensor_copy, heads(qp[0:n], ROPE), qbuf[0:n, :, NOPE:])
                rotated_key(kp2n[0:n, 0:32], n)
                do_signal(s_q_ready, 1, dve.tensor_tensor, kp2n[0:n, 32:64], lat[0:n, QR + KVR:], lat[0:n, QR + KVR:], ALU.mult)
                dve.wait_ge(s_q_ps, 1)
                do(dve.tensor_copy, qnT[:].rearrange("p r t -> p (r t)"), bank(0, P, 128))
                for b in range(SEQS):
                    do(dve.tensor_copy, QPT[0:32, b], bank(1, 32, 256).rearrange("p (h b s) -> p h b s", h=H, b=SEQS)[:, :, b, :])
                do_signal(s_q_copied, 1, dve.tensor_copy, kpTn[0:64], bank(2, 64, 32))
                dve.wait_ge(s_ql_ps, 1)
                for b in range(SEQS):
                    for a in range(2):
                        src = bank(2 + a, P, 128).rearrange("p (h b s) -> p h b s", h=4, b=SEQS)[:, :, b, :]
                        if (b, a) != (SEQS - 1, 1):
                            do(dve.tensor_copy, half(QT[:, b], a), src)
                        else:
                            do_signal(s_ql_ready, 1, dve.tensor_copy, half(QT[:, b], a), src)

            def sample_retention():
                t, n = TILES, ST
                dve.wait_ge(inner_ps, t + 1)
                for g, b in ((0, 0), (1, 5)):
                    src = heads(bank(b, n), P)[:, :, 0:n]
                    dmat = half(dec_in_s[0:n].rearrange("p (h i) -> p h i", h=H), g)
                    own.wait()
                    ins = dve.tensor_tensor(half(inT[0:n], g)[:, :, 0:n], src, dmat, ALU.mult)
                    if g == 0:
                        own.done(ins)
                    else:
                        own.raises(ins, inner_ready, t + 1)
                for h in range(H):
                    dve.wait_ge(s_cross_ps, h + 1)
                    own_part = heads(osq[0:n])
                    do_signal(s_cross_taken, h + 1, dve.tensor_tensor, own_part, heads(bank(2 + h % 2, n)),
                              over(cross_s[0:n, h], 2, [n, SEQS, 64]), ALU.mult)
                    do(dve.tensor_reduce, crossv[0:n, h * 64:(h + 1) * 64], own_part.rearrange("p b v -> p v b"), AX_X, ALU.add)
                for h in range(H):
                    if h >= 2:
                        dve.wait_ge(s_R_ps, h - 1)
                    do_signal(s_vexp, h + 1, dve.tensor_tensor, heads(mix[0:n, (h % 2) * 512:(h % 2 + 1) * 512]),
                              over(rv[0:n, h * 64:(h + 1) * 64], 1, [n, SEQS, 64]), over(same_s[0:n], 2, [n, SEQS, 64]), ALU.mult)
                    if h % 2 == 1:
                        r = h // 2
                        dve.wait_ge(s_R_ps, h + 1)
                        st = Rs[:, r].rearrange("p b v -> p (b v)")
                        do_signal(s_R_ready, r + 1, dve.scalar_tensor_tensor, out=st, in0=st, scalar=dec_state_s[:, r:r + 1],
                                  in1=bank(5), op0=ALU.mult, op1=ALU.add)
                dve.wait_ge(o_ps, t + 1)
                do_signal(o_taken, t + 1, dve.tensor_tensor, oret[0:n], bank(1, n), crossv[0:n], ALU.add)
                group_norm(n, lambda: None)

            def sample_sequence(b):
                dve.wait_ge(pages_in[b % 2], 16 * 2 * PAGES * (b // 2 + 1))
                raw = pg[:, b % 2, :, KVR:]
                do(dve.tensor_tensor, kp2[:, :, 32:64], raw, over(k_wb[:, NOPE:], 1, [P, PAGES, ROPE]), ALU.mult)
                rotate(kp2[:, :, 0:32], kp2[:, :, 32:64], rpages[:, :, 0:32], rpages[:, :, 32:64], kpt, [P, PAGES, ROPE])
                do_signal(kp2_ready, b + 1, dve.tensor_tensor, kp2[:, :, 32:64], raw, raw, ALU.mult)
                dve.wait_ge(pageT_ps, b + 1)
                do(dve.tensor_copy, kpT[0:64, 0:512], bank(2, 64))
                do_signal(kpT_ready, b + 1, dve.tensor_copy, kpT[0:64, 512:1024], bank(3, 64))
                for j in range(PAGES + 1):
                    m = (PAGES + 1) * b + j
                    n = P if j < PAGES else STEPS
                    dve.wait_ge(kn_sq, m + 1)
                    do_signal(kn_taken, m + 1, dve.tensor_reduce, ss_k[0:n, j * 8:(j + 1) * 8], heads(sqn[0:n, m % 2, :]), AX_X, ALU.add)
                dve.wait_ge(sT_ps, b + 1)
                do(dve.tensor_tensor, ss_k[:, 0:64], ss_k[:, 0:64], bank(1, P, 64), ALU.add)
                do(dve.tensor_tensor, ss_k[0:STEPS, 64:72], ss_k[0:STEPS, 64:72], ps[0:STEPS, 3, 64:72], ALU.add)
                do(dve.tensor_scalar, root_x[:, 0:72], ss_k, 1.0 / QK, EPS, ALU.mult, ALU.add)
                root(P, 72)
                do(dve.tensor_tensor, heads(sT[:, 0:256], STEPS), heads(bank(0, P, 256), STEPS),
                   over(root_y[:, 0:64], 2, [P, 64, STEPS]), ALU.mult)
                do_signal(sT_ready, b + 1, dve.tensor_tensor, heads(sT[0:STEPS, 256:288], STEPS), heads(ps[0:STEPS, 2, 256:288], STEPS),
                          over(root_y[0:STEPS, 64:72], 2, [STEPS, H, STEPS]), ALU.mult)
                dve.wait_ge(s_ps, b + 1)
                do(dve.tensor_reduce, smx[0:32, 0:1], ps[0:32, 4:6, :].rearrange("p a b -> p (a b)"), AX_X, ALU.max)
                do(dve.tensor_tensor, s4[0:32], bank(4, 32, STEPS), mask4[0:32], ALU.add)
                do(dve.tensor_reduce, smx[0:32, 1:2], s4[0:32], AX_X, ALU.max)
                do(dve.tensor_tensor, smx[0:32, 2:3], smx[0:32, 0:1], smx[0:32, 1:2], ALU.max)
                do_signal(s_max, b + 1, dve.tensor_scalar, smx[0:32, 3:4], smx[0:32, 2:3], -SCALE, None, ALU.mult)
                dve.wait_ge(s_pT_ps, b + 1)
                do(dve.tensor_copy, pT[:, 0:256], bank(0, P, 256))
                do_signal(s_pT, b + 1, dve.tensor_copy, pT[0:STEPS, 256:288], ps[0:STEPS, 2, 256:288])
                dve.wait_ge(s_prob, b + 1)
                do(dve.tensor_tensor, smx[0:32, 6:7], smx[0:32, 4:5], smx[0:32, 5:6], ALU.add)
                do(dve.reciprocal, smx[0:32, 6:7], smx[0:32, 6:7])
                dve.wait_ge(s_o_ps, b + 1)
                do_signal(s_o, b + 1, dve.tensor_scalar, ol[0:32], bank(1, 32, KVR), smx[0:32, 6:7], None, ALU.mult)
                dve.wait_ge(s_oT_ps, b + 1)
                do_signal(s_oT, b + 1, dve.tensor_copy, OL[:, :, b, :], heads(bank(2, P, 32), STEPS))

            def sample_front(slots):
                t, n = TILES, ST
                do(dve.memset, ss_k[:], 1.0)
                do_signal(s_set, 1, dve.memset, ones32[:], 1.0)
                project(t, n, slots)
                dve.wait_ge(s_const_in, 16 * 7)
                sample_queries()
                slots()
                sample_retention()
                slots()
                for b in range(SEQS):
                    sample_sequence(b)
                    slots()
                dve.wait_ge(piece_done, PIECES * t + O_0)
                do_signal(wide_ready, 3 * t + 2, dve.tensor_copy, mix[0:n, 0:512], bank(0, n))
                out_and_peer(t, n, slots)

            dve.wait_ge(const_in, 16 * N_CONST)
            dve.wait_ge(const_set, 1)
            do(dve.tensor_scalar, ret_wb[:], ret_wb[:], 0.5, None, ALU.mult)
            do(dve.memset, kT[:], 0.0)
            do(dve.memset, vN[:], 0.0)
            do_signal(R_ready, 1, dve.memset, R[:], 0.0)
            prompt_front(0, lambda: None)
            hand_numbers(0, P)
            hand_rows(0, P)
            hand_h(0, P)
            own.close()
            with dve.Fori(1, TILES) as i:
                prompt_front(i, Between(expert_slots, i - 1, prompt_slots(), P))
                hand_numbers(i, P)
                make_coefs(i - 1, SLOTS - 2, P)
                hand_rows(i, P)
                finish(i - 1, P)
                hand_h(i, P)
                own.close()
            sample_front(Between(expert_slots, TILES - 1, sample_slots(), P))
            hand_numbers(TILES, ST)
            make_coefs(TILES - 1, SLOTS - 2, P)
            hand_rows(TILES, ST)
            finish(TILES - 1, P)
            hand_h(TILES, ST)
            expert_slots(TILES, 0, SLOTS, ST)
            make_coefs(TILES, SLOTS - 2, ST)
            finish(TILES, ST)


class Between:

    def __init__(self, expert_slots, t, sizes, n, behind=False):
        assert sum(sizes) == SLOTS and all(s % 2 == 0 and s >= 0 for s in sizes), sizes
        self.expert_slots, self.t, self.n, self.step = expert_slots, t, n, 0
        bounds = [sum(sizes[:i]) for i in range(len(sizes) + 1)]
        if behind:
            bounds = [max(b - 2, 0) for b in bounds] + [SLOTS]
        self.bounds = bounds

    def __call__(self):
        self.expert_slots(self.t, *self.bounds[self.step:self.step + 2], self.n)
        self.step += 1

    def rest(self):
        self()
        assert self.step == len(self.bounds) - 1, (self.step, len(self.bounds))


def shape_constants():
    import numpy as np

    f = np.float32

    def rope(pos, width):
        half = width // 2
        inv = (f(10000.0) ** (-np.arange(half, dtype=f) / f(half))).astype(f)
        ang = pos.astype(f)[:, None] * inv[None, :]
        c, s = np.cos(ang).astype(f), np.sin(ang).astype(f)
        return np.concatenate([c, c, -s, s], 1)

    pos = np.concatenate([np.arange(TILES * P), TILES * P + np.tile(np.arange(STEPS), SEQS)])
    rope_rows = np.concatenate([rope(pos, ROPE), rope(pos, 64)], 1)
    rope_pages = rope(np.arange(PAGES * P), ROPE).reshape(PAGES, P, 64).transpose(1, 0, 2)
    q, c = np.arange(P)[:, None], np.arange((2 * TILES - 1) * P)[None, :]
    mask_rows = np.where(c - (TILES - 1) * P <= q, 0.0, -1e30).astype(f)
    mask_new = np.where(np.arange(STEPS)[None, :] <= (np.arange(ST) % STEPS)[:, None], 0.0, -1e30).astype(f)
    lg = np.log1p(-np.power(f(2.0), f(-5.0) - np.arange(H, dtype=f))).astype(f)

    def inner(c):
        i = np.arange(c, dtype=f)
        diff = i[None, :] - i[:, None]
        return np.where(diff[None] >= 0, np.exp(lg[:, None, None] * np.maximum(diff, 0)[None]), 0).astype(f)

    def pairs(a):
        return np.repeat(a.reshape(4, 2).T, 64, 0)

    i = np.arange(P, dtype=f)
    s = (np.arange(ST) % STEPS).astype(f)
    seq = np.arange(ST) // STEPS
    same = (seq[:, None] == np.arange(SEQS)[None, :]).astype(f)
    within = inner(STEPS)
    s_in = np.zeros((ST, H, ST), f)
    for b in range(SEQS):
        r = slice(b * STEPS, (b + 1) * STEPS)
        s_in[r, :, r] = within.transpose(1, 0, 2)
    out = dict(
        rope_rows=rope_rows, rope_pages=rope_pages, mask_rows=mask_rows, mask_new=mask_new,
        decay_in=inner(P).transpose(1, 0, 2), decay_cross=np.exp(lg[None] * (i[:, None] + 1)),
        decay_k=np.exp(lg[None] * (P - 1 - i[:, None])) * f(0.125), decay_state=pairs(np.exp(lg * P)),
        s_decay_in=s_in.reshape(ST, H * ST), s_decay_cross=np.exp(lg[None, :, None] * (s[:, None, None] + 1)) * same[:, None, :],
        s_decay_k=np.exp(lg[None] * (STEPS - 1 - s[:, None])) * f(0.125), s_decay_state=pairs(np.exp(lg * STEPS)),
        s_same=same, eye=np.eye(P),
    )
    return {k: np.ascontiguousarray(v, dtype=f) for k, v in out.items()}


def kernel(x_prompt, x_sample, cache_kv_latent, cache_k_rope, state_ret, page_table, attn_norm_w, w_in,
           q_a_norm_w, w_uq, q_norm_w, kv_a_norm_w, w_ukv, k_norm_w, ret_norm_w, w_o, ffn_norm_w, w_peer_q,
           peer_sub_keys1, peer_sub_keys2, peer_u, peer_v):
    import numpy as np
    import concourse.bacc as bacc
    from concourse.bass_utils import run_bass_kernel_spmd

    def chunks(w):
        return w.reshape(-1, P, w.shape[-1]).transpose(1, 0, 2)

    wi = np.asarray(w_in)[0]
    room = np.zeros((D, 2 * PIECE - LAT), wi.dtype)
    def pieces(w):
        return w.reshape(DC, P, -1, PIECE).transpose(2, 1, 0, 3).reshape(-1, P, DC * PIECE)

    def one_piece(w):
        return np.concatenate([w, np.zeros((P, DC * PIECE - w.shape[1]), w.dtype)], 1)[None]

    ukv = np.asarray(w_ukv)[0].reshape(KVR, H, 2, 64)
    w_uk, w_uv = ukv[:, :, 0].reshape(KVR, 512), ukv[:, :, 1].reshape(KVR, 512)
    w = np.concatenate([
        pieces(np.concatenate([wi[:, :LAT], room, wi[:, LAT:]], 1)),
        one_piece(chunks(np.asarray(w_uq)[0]).reshape(P, 2 * 768)), one_piece(np.concatenate([w_uk, w_uv], 1)),
        pieces(np.asarray(w_o)[0]), pieces(np.asarray(w_peer_q)[0])])
    ins = dict(
        x_prompt=np.asarray(x_prompt)[0], x_sample=np.asarray(x_sample).reshape(ST, D),
        cache_latent=np.asarray(cache_kv_latent)[0], cache_rope=np.asarray(cache_k_rope)[0],
        state=np.asarray(state_ret)[0], page_table=np.asarray(page_table).reshape(1, SEQS * PAGES),
        attn_w=np.asarray(attn_norm_w)[0].reshape(DC, P).T, weights=w,
        qa_w=np.asarray(q_a_norm_w)[0].reshape(2, P).T,
        q_w=np.asarray(q_norm_w)[0], kva_w=np.asarray(kv_a_norm_w)[0],
        w_ukT=w_uk.T.reshape(4, P, KVR).transpose(1, 0, 2), k_w=np.asarray(k_norm_w)[0],
        ret_w=np.asarray(ret_norm_w)[0], ffn_w=np.asarray(ffn_norm_w)[0],
        keys1T=np.asarray(peer_sub_keys1)[0].T, keys2T=np.asarray(peer_sub_keys2)[0].T,
        experts=np.concatenate([np.asarray(peer_u)[0], np.asarray(peer_v)[0]], 1),
    )
    ins.update(shape_constants())
    outs = dict(y_prompt=(TILES * P, D), y_sample=(ST, D), lat_prompt=(TILES * P, KVR), pe_prompt=(TILES * P, ROPE),
                R_prompt=(H, 64, 64), lat_sample=(ST, KVR), pe_sample=(ST, ROPE), R_sample=(SEQS, H, 64, 64))
    nc = bacc.Bacc("TRN2", target_bir_lowering=False, num_devices=1)
    arrays, args = {}, []
    for name, a in ins.items():
        arrays[name] = np.ascontiguousarray(a)
        args.append(nc.dram_tensor(name, a.shape, mybir.dt.from_np(a.dtype), kind="ExternalInput").ap())
    for name, shape in outs.items():
        args.append(nc.dram_tensor(name, shape, F32, kind="ExternalOutput").ap())
    hybrid_decoder_step(nc, *args)
    r = run_bass_kernel_spmd(nc, [arrays], core_ids=[0]).results[0]
    return (r["y_prompt"].reshape(1, TILES * P, D), r["y_sample"].reshape(SEQS, STEPS, D),
            r["lat_prompt"].reshape(1, 1, TILES * P, KVR), r["pe_prompt"].reshape(1, 1, TILES * P, ROPE),
            r["R_prompt"].reshape(1, 1, H, 64, 64), r["lat_sample"].reshape(1, SEQS, STEPS, KVR),
            r["pe_sample"].reshape(1, SEQS, STEPS, ROPE), r["R_sample"].reshape(1, SEQS, H, 64, 64))
```
